# Optimizing a Trainium2 kernel written in Bass

```python
import math
import numpy as np
import jax
import jax.numpy as jnp
from jax import lax

D_MODEL = 1024
BATCH = 1
SEQ = 256
DEPTH = 2

HEAD_DIM = 64
Q_BLOCK = 128
ROPE_THETA = 10000.0
NORM_EPS = 1e-6
NEG_INF = -1e30
MACARON_WEIGHT = 0.5
FFN_DIM = 2816
MEM_LEN = 256
XA_HEADS = 4
XA_HEAD_DIM = D_MODEL // XA_HEADS

MLA_HEADS = 4
MLA_Q_LORA = 192
MLA_KV_LORA = 128
MLA_NOPE_DIM = 64
MLA_ROPE_DIM = 32
MLA_V_DIM = 64

NSA_HEADS = 4
NSA_CMP_LEN = 32
NSA_CMP_STRIDE = 16
NSA_CMP_HIDDEN = 256
NSA_SEL_LEN = 64
NSA_SEL_BLOCKS = 8
NSA_SEL_Q_BLOCK = 64
NSA_WINDOW = 256
NSA_FORCE_SCORE = 1e4

FOX_HEADS = 4

S5_WIDTH = 256
S5_GROUP = 16
S5_GROUPS = S5_WIDTH // S5_GROUP
S5_STATE = 64
S5_DT_MIN = 1e-3
S5_DT_MAX = 1e-1

N_MIXERS = 4
GROUP_WIDTH = 256
MIX_WIDTH = N_MIXERS * GROUP_WIDTH
MLA_IN = MLA_Q_LORA + MLA_KV_LORA + MLA_ROPE_DIM
NSA_IN = NSA_HEADS * HEAD_DIM + 6 * HEAD_DIM + 3 * NSA_HEADS
FOX_IN = 3 * FOX_HEADS * HEAD_DIM + FOX_HEADS
S5_IN = S5_WIDTH
IN_WIDTH = MLA_IN + NSA_IN + FOX_IN + S5_IN

kernel_name = 'hybrid_parallel_mla_nsa_fox_s5_block'

def _rmsnorm(x, g):
    xf = x.astype(jnp.float32)
    y = xf * lax.rsqrt(jnp.mean(xf * xf, axis=-1, keepdims=True) + NORM_EPS)
    return (y * g.astype(jnp.float32)).astype(x.dtype)

def _rope_tables(n, dim):
    inv = 1.0 / (ROPE_THETA ** (jnp.arange(0, dim, 2, dtype=jnp.float32) / dim))
    ang = jnp.arange(n, dtype=jnp.float32)[:, None] * inv[None, :]
    return jnp.cos(ang), jnp.sin(ang)

def _rope(x, cos, sin):
    c = cos[:, None, :].astype(x.dtype)
    s = sin[:, None, :].astype(x.dtype)
    x1, x2 = jnp.split(x, 2, axis=-1)
    return jnp.concatenate([x1 * c - x2 * s, x1 * s + x2 * c], axis=-1)

def _masked_softmax(s, mask):
    s = jnp.where(mask, s, NEG_INF)
    m = jnp.max(s, axis=-1, keepdims=True)
    e = jnp.where(mask, jnp.exp(s - m), 0.0)
    return e / jnp.maximum(jnp.sum(e, axis=-1, keepdims=True), 1e-30)

def _swiglu(x, w_gate, w_up, w_down):
    return (jax.nn.silu(x @ w_gate) * (x @ w_up)) @ w_down

def _causal_block_attention(q, k, v, scale, cum_log_f=None):
    S = q.shape[1]
    pos = jnp.arange(S)
    cum_t = None if cum_log_f is None else jnp.transpose(cum_log_f, (0, 2, 1))
    outs = []
    for i in range(S // Q_BLOCK):
        lo, hi = i * Q_BLOCK, (i + 1) * Q_BLOCK
        s = jnp.einsum('bqhd,bkhd->bhqk', q[:, lo:hi], k[:, :hi]).astype(jnp.float32) * scale
        if cum_t is not None:
            s = s + cum_t[:, :, lo:hi, None] - cum_t[:, :, None, :hi]
        mask = pos[lo:hi, None] >= pos[None, :hi]
        p = _masked_softmax(s, mask)
        outs.append(jnp.einsum('bhqk,bkhd->bqhd', p.astype(v.dtype), v[:, :hi]))
    return jnp.concatenate(outs, axis=1)

def _mla(c_q, c_kv, k_pe, q_norm_g, w_uq, kv_norm_g, w_ukv, rope):
    B, S, _ = c_q.shape
    H = MLA_HEADS
    q = (_rmsnorm(c_q, q_norm_g) @ w_uq).reshape(B, S, H, MLA_NOPE_DIM + MLA_ROPE_DIM)
    q = jnp.concatenate([q[..., :MLA_NOPE_DIM], _rope(q[..., MLA_NOPE_DIM:], *rope)], axis=-1)
    kv = (_rmsnorm(c_kv, kv_norm_g) @ w_ukv).reshape(B, S, H, MLA_NOPE_DIM + MLA_V_DIM)
    k_pe = jnp.broadcast_to(_rope(k_pe[:, :, None, :], *rope), (B, S, H, MLA_ROPE_DIM))
    k = jnp.concatenate([kv[..., :MLA_NOPE_DIM], k_pe], axis=-1)
    o = _causal_block_attention(q, k, kv[..., MLA_NOPE_DIM:], (MLA_NOPE_DIM + MLA_ROPE_DIM) ** -0.5)
    return o.reshape(B, S, H * MLA_V_DIM)

def _nsa(q, k_cmp, v_cmp, k_slc, v_slc, k_swa, v_swa, gate_logit, cmp_pos, phi_w1, phi_b1, phi_w2, gate_b, rope):
    B, S, _ = q.shape
    H, d = NSA_HEADS, HEAD_DIM
    scale = d ** -0.5
    pos = jnp.arange(S)
    q = _rope(q.reshape(B, S, H, d), *rope)

    def rope1(t):
        return _rope(t[:, :, None, :], *rope)[:, :, 0, :]

    k_cmp, k_slc, k_swa = rope1(k_cmp), rope1(k_slc), rope1(k_swa)

    n_cmp = (S - NSA_CMP_LEN) // NSA_CMP_STRIDE + 1
    blk_idx = np.arange(n_cmp)[:, None] * NSA_CMP_STRIDE + np.arange(NSA_CMP_LEN)[None, :]

    def compress(t, j):
        blocks = t[:, blk_idx] + cmp_pos[j]
        hid = jax.nn.gelu(blocks.reshape(B, n_cmp, NSA_CMP_LEN * d) @ phi_w1[j] + phi_b1[j])
        return hid @ phi_w2[j]

    kc, vc = compress(k_cmp, 0), compress(v_cmp, 1)
    cmp_end = jnp.arange(n_cmp) * NSA_CMP_STRIDE + NSA_CMP_LEN - 1
    s_c = jnp.einsum('bshd,bcd->bhsc', q, kc).astype(jnp.float32) * scale
    p_c = _masked_softmax(s_c, pos[:, None] >= cmp_end[None, :])
    o_cmp = jnp.einsum('bhsc,bcd->bshd', p_c.astype(vc.dtype), vc)

    n_blk = S // NSA_SEL_LEN
    n_sel = min(NSA_SEL_BLOCKS, n_blk)
    cs = np.arange(n_cmp) * NSA_CMP_STRIDE
    ss = np.arange(n_blk) * NSA_SEL_LEN
    overlap = ((cs[:, None] < ss[None, :] + NSA_SEL_LEN) & (cs[:, None] + NSA_CMP_LEN > ss[None, :])).astype(np.float32)
    imp = jnp.einsum('bhsc,cj->bsj', p_c, jnp.asarray(overlap))
    blk = jnp.arange(n_blk)[None, :]
    cur = (pos // NSA_SEL_LEN)[:, None]
    forced = (blk == 0) | (blk == cur) | (blk == cur - 1)
    score = jnp.where(forced, NSA_FORCE_SCORE, imp)
    score = jnp.where(blk <= cur, score, NEG_INF)
    _, sel_idx = lax.top_k(score, n_sel)

    kb = k_slc.reshape(B, n_blk, NSA_SEL_LEN, d)
    vb = v_slc.reshape(B, n_blk, NSA_SEL_LEN, d)
    nqb = S // NSA_SEL_Q_BLOCK
    q_blocks = q.reshape(B, nqb, NSA_SEL_Q_BLOCK, H, d).transpose(1, 0, 2, 3, 4)
    idx_blocks = sel_idx.reshape(B, nqb, NSA_SEL_Q_BLOCK, n_sel).transpose(1, 0, 2, 3)
    t_blocks = pos.reshape(nqb, NSA_SEL_Q_BLOCK)
    n_keys = n_sel * NSA_SEL_LEN

    def sel_attend(args):
        qb, ib, tb = args
        ks = jax.vmap(lambda kk, ii: kk[ii])(kb, ib)
        vs = jax.vmap(lambda vv, ii: vv[ii])(vb, ib)
        kpos = ib[..., None] * NSA_SEL_LEN + jnp.arange(NSA_SEL_LEN)
        mask = (kpos <= tb[None, :, None, None]).reshape(B, 1, NSA_SEL_Q_BLOCK, n_keys)
        s = jnp.einsum('bqhd,bqnld->bhqnl', qb, ks).astype(jnp.float32).reshape(B, H, NSA_SEL_Q_BLOCK, n_keys) * scale
        p = _masked_softmax(s, mask)
        return jnp.einsum('bhqm,bqmd->bqhd', p.astype(vs.dtype), vs.reshape(B, NSA_SEL_Q_BLOCK, n_keys, d))

    o_slc = lax.map(sel_attend, (q_blocks, idx_blocks, t_blocks))
    o_slc = o_slc.transpose(1, 0, 2, 3, 4).reshape(B, S, H, d)

    nqw = S // Q_BLOCK
    n_prev = NSA_WINDOW // Q_BLOCK
    pad = ((0, 0), (NSA_WINDOW, 0), (0, 0))
    kp = jnp.pad(k_swa, pad).reshape(B, nqw + n_prev, Q_BLOCK, d)
    vp = jnp.pad(v_swa, pad).reshape(B, nqw + n_prev, Q_BLOCK, d)
    kw = jnp.concatenate([kp[:, o:o + nqw] for o in range(n_prev + 1)], axis=2)
    vw = jnp.concatenate([vp[:, o:o + nqw] for o in range(n_prev + 1)], axis=2)
    qpos = pos.reshape(nqw, Q_BLOCK)
    kpos = (jnp.arange(nqw) * Q_BLOCK - NSA_WINDOW)[:, None] + jnp.arange((n_prev + 1) * Q_BLOCK)[None, :]
    kq = kpos[:, None, :]
    tq = qpos[:, :, None]
    wmask = (kq <= tq) & (kq > tq - NSA_WINDOW) & (kq >= 0)
    s_w = jnp.einsum('bnqhd,bnkd->bnhqk', q.reshape(B, nqw, Q_BLOCK, H, d), kw).astype(jnp.float32) * scale
    p_w = _masked_softmax(s_w, wmask[None, :, None])
    o_swa = jnp.einsum('bnhqk,bnkd->bnqhd', p_w.astype(vw.dtype), vw).reshape(B, S, H, d)

    g = jax.nn.sigmoid((gate_logit + gate_b).astype(jnp.float32)).reshape(B, S, 3, H)
    out = g[:, :, 0, :, None] * o_cmp + g[:, :, 1, :, None] * o_slc + g[:, :, 2, :, None] * o_swa
    return out.reshape(B, S, H * d).astype(q.dtype)

def _fox(q, k, v, f_logit, f_b):
    B, S, _ = q.shape
    shp = (B, S, FOX_HEADS, HEAD_DIM)
    log_f = jax.nn.log_sigmoid((f_logit + f_b).astype(jnp.float32))
    cum = jnp.cumsum(log_f, axis=1)
    o = _causal_block_attention(q.reshape(shp), k.reshape(shp), v.reshape(shp), HEAD_DIM ** -0.5, cum)
    return o.reshape(B, S, FOX_HEADS * HEAD_DIM)

def _s5(u, lam_re, lam_im, log_dt, b_re, b_im, c_re, c_im, d_skip, glu_w, glu_b):
    B, S, _ = u.shape
    f32 = jnp.float32
    uf = u.astype(f32).reshape(B, S, S5_GROUPS, S5_GROUP)
    dt = jnp.exp(log_dt.astype(f32))[:, None]
    lr, li = lam_re.astype(f32), lam_im.astype(f32)
    mag = jnp.exp(lr * dt)
    ar, ai = mag * jnp.cos(li * dt), mag * jnp.sin(li * dt)
    den = lr * lr + li * li
    kr = ((ar - 1.0) * lr + ai * li) / den
    ki = (ai * lr - (ar - 1.0) * li) / den
    bu_r = jnp.einsum('bsgc,gpc->bsgp', uf, b_re.astype(f32))
    bu_i = jnp.einsum('bsgc,gpc->bsgp', uf, b_im.astype(f32))
    br = kr * bu_r - ki * bu_i
    bi = kr * bu_i + ki * bu_r
    a_r = jnp.broadcast_to(ar, (1, S, S5_GROUPS, S5_STATE))
    a_i = jnp.broadcast_to(ai, (1, S, S5_GROUPS, S5_STATE))

    def combine(e1, e2):
        a1r, a1i, b1r, b1i = e1
        a2r, a2i, b2r, b2i = e2
        return (a2r * a1r - a2i * a1i, a2r * a1i + a2i * a1r,
                a2r * b1r - a2i * b1i + b2r, a2r * b1i + a2i * b1r + b2i)

    _, _, xr, xi = lax.associative_scan(combine, (a_r, a_i, br, bi), axis=1)
    y = (jnp.einsum('bsgp,gcp->bsgc', xr, c_re.astype(f32))
         - jnp.einsum('bsgp,gcp->bsgc', xi, c_im.astype(f32))
         + d_skip.astype(f32) * uf)
    y = jax.nn.gelu(y.reshape(B, S, S5_WIDTH))
    out = y * jax.nn.sigmoid(y @ glu_w.astype(f32) + glu_b.astype(f32))
    return out.astype(u.dtype)

def _token_mixing(u, w_in, mla_q_norm_g, mla_w_uq, mla_kv_norm_g, mla_w_ukv,
                  nsa_cmp_pos, nsa_phi_w1, nsa_phi_b1, nsa_phi_w2, nsa_gate_b, fox_f_b,
                  s5_lambda_re, s5_lambda_im, s5_log_dt, s5_b_re, s5_b_im, s5_c_re, s5_c_im,
                  s5_d, s5_glu_w, s5_glu_b, group_g, w_out, rope_mla, rope_nsa):
    B, S, _ = u.shape
    proj = u @ w_in
    p_mla, p_nsa, p_fox, p_s5 = jnp.split(proj, [MLA_IN, MLA_IN + NSA_IN, MLA_IN + NSA_IN + FOX_IN], axis=-1)
    c_q, c_kv, k_pe = jnp.split(p_mla, [MLA_Q_LORA, MLA_Q_LORA + MLA_KV_LORA], axis=-1)
    o_mla = _mla(c_q, c_kv, k_pe, mla_q_norm_g, mla_w_uq, mla_kv_norm_g, mla_w_ukv, rope_mla)
    nq = NSA_HEADS * HEAD_DIM
    q_n, kc, vc, ksl, vsl, kw, vw, g_n = jnp.split(p_nsa, [nq + i * HEAD_DIM for i in range(7)], axis=-1)
    o_nsa = _nsa(q_n, kc, vc, ksl, vsl, kw, vw, g_n, nsa_cmp_pos, nsa_phi_w1, nsa_phi_b1, nsa_phi_w2, nsa_gate_b, rope_nsa)
    fw = FOX_HEADS * HEAD_DIM
    q_f, k_f, v_f, f_f = jnp.split(p_fox, [fw, 2 * fw, 3 * fw], axis=-1)
    o_fox = _fox(q_f, k_f, v_f, f_f, fox_f_b)
    o_s5 = _s5(p_s5, s5_lambda_re, s5_lambda_im, s5_log_dt, s5_b_re, s5_b_im, s5_c_re, s5_c_im, s5_d, s5_glu_w, s5_glu_b)
    y = jnp.stack([o_mla, o_nsa, o_fox, o_s5], axis=2)
    y = _rmsnorm(y, group_g).reshape(B, S, MIX_WIDTH)
    return y @ w_out

def _cross_attention(h, mem_n, w_q, w_kv, w_o):
    B, S, _ = h.shape
    M = mem_n.shape[1]
    q = (h @ w_q).reshape(B, S, XA_HEADS, XA_HEAD_DIM)
    kv = (mem_n @ w_kv).reshape(B, M, 2, XA_HEADS, XA_HEAD_DIM)
    s = jnp.einsum('bshd,bmhd->bhsm', q, kv[:, :, 0]).astype(jnp.float32) * XA_HEAD_DIM ** -0.5
    p = jax.nn.softmax(s, axis=-1)
    o = jnp.einsum('bhsm,bmhd->bshd', p.astype(kv.dtype), kv[:, :, 1]).reshape(B, S, XA_HEADS * XA_HEAD_DIM)
    return o @ w_o

def setup_inputs(seed: int = 0) -> dict:
    key = jax.random.key(seed)
    ks = iter(jax.random.split(key, 64))
    f32 = jnp.float32
    L, G, P = DEPTH, S5_GROUPS, S5_STATE

    def nrm(shape, scale):
        return jax.random.normal(next(ks), shape, f32) * scale

    def gain(shape):
        return 1.0 + 0.02 * jax.random.normal(next(ks), shape, f32)

    n_idx = jnp.arange(P, dtype=f32)
    return {
        'x': nrm((BATCH, SEQ, D_MODEL), 1.0),
        'mem': nrm((BATCH, MEM_LEN, D_MODEL), 1.0),
        'ffn1_pre_g': gain((L, D_MODEL)),
        'ffn1_w_gate': nrm((L, D_MODEL, FFN_DIM), D_MODEL ** -0.5),
        'ffn1_w_up': nrm((L, D_MODEL, FFN_DIM), D_MODEL ** -0.5),
        'ffn1_w_down': nrm((L, FFN_DIM, D_MODEL), FFN_DIM ** -0.5),
        'ffn1_post_g': gain((L, D_MODEL)),
        'mix_pre_g': gain((L, D_MODEL)),
        'mix_w_in': nrm((L, D_MODEL, IN_WIDTH), D_MODEL ** -0.5),
        'mla_q_norm_g': gain((L, MLA_Q_LORA)),
        'mla_w_uq': nrm((L, MLA_Q_LORA, MLA_HEADS * (MLA_NOPE_DIM + MLA_ROPE_DIM)), MLA_Q_LORA ** -0.5),
        'mla_kv_norm_g': gain((L, MLA_KV_LORA)),
        'mla_w_ukv': nrm((L, MLA_KV_LORA, MLA_HEADS * (MLA_NOPE_DIM + MLA_V_DIM)), MLA_KV_LORA ** -0.5),
        'nsa_cmp_pos': nrm((L, 2, NSA_CMP_LEN, HEAD_DIM), 0.1),
        'nsa_phi_w1': nrm((L, 2, NSA_CMP_LEN * HEAD_DIM, NSA_CMP_HIDDEN), (NSA_CMP_LEN * HEAD_DIM) ** -0.5),
        'nsa_phi_b1': nrm((L, 2, NSA_CMP_HIDDEN), 0.02),
        'nsa_phi_w2': nrm((L, 2, NSA_CMP_HIDDEN, HEAD_DIM), NSA_CMP_HIDDEN ** -0.5),
        'nsa_gate_b': nrm((L, 3 * NSA_HEADS), 0.02),
        'fox_f_b': 2.0 + nrm((L, FOX_HEADS), 0.5),
        's5_lambda_re': -0.5 * (1.0 + nrm((L, G, P), 0.01)),
        's5_lambda_im': jnp.pi * n_idx * (1.0 + nrm((L, G, P), 0.01)),
        's5_log_dt': jax.random.uniform(next(ks), (L, G), f32, math.log(S5_DT_MIN), math.log(S5_DT_MAX)),
        's5_b_re': nrm((L, G, P, S5_GROUP), S5_GROUP ** -0.5),
        's5_b_im': nrm((L, G, P, S5_GROUP), S5_GROUP ** -0.5),
        's5_c_re': nrm((L, G, S5_GROUP, P), P ** -0.5),
        's5_c_im': nrm((L, G, S5_GROUP, P), P ** -0.5),
        's5_d': nrm((L, G, S5_GROUP), 0.1),
        's5_glu_w': nrm((L, S5_WIDTH, S5_WIDTH), S5_WIDTH ** -0.5),
        's5_glu_b': nrm((L, S5_WIDTH), 0.02),
        'mix_group_g': gain((L, N_MIXERS, GROUP_WIDTH)),
        'mix_w_out': nrm((L, MIX_WIDTH, D_MODEL), MIX_WIDTH ** -0.5),
        'mix_post_g': gain((L, D_MODEL)),
        'xa_pre_g': gain((L, D_MODEL)),
        'xa_mem_g': gain((L, D_MODEL)),
        'xa_w_q': nrm((L, D_MODEL, XA_HEADS * XA_HEAD_DIM), D_MODEL ** -0.5),
        'xa_w_kv': nrm((L, D_MODEL, 2 * XA_HEADS * XA_HEAD_DIM), D_MODEL ** -0.5),
        'xa_w_o': nrm((L, XA_HEADS * XA_HEAD_DIM, D_MODEL), (XA_HEADS * XA_HEAD_DIM) ** -0.5),
        'xa_post_g': gain((L, D_MODEL)),
        'ffn2_pre_g': gain((L, D_MODEL)),
        'ffn2_w_gate': nrm((L, D_MODEL, FFN_DIM), D_MODEL ** -0.5),
        'ffn2_w_up': nrm((L, D_MODEL, FFN_DIM), D_MODEL ** -0.5),
        'ffn2_w_down': nrm((L, FFN_DIM, D_MODEL), FFN_DIM ** -0.5),
        'ffn2_post_g': gain((L, D_MODEL)),
    }

def reference(x, mem, ffn1_pre_g, ffn1_w_gate, ffn1_w_up, ffn1_w_down, ffn1_post_g,
              mix_pre_g, mix_w_in, mla_q_norm_g, mla_w_uq, mla_kv_norm_g, mla_w_ukv,
              nsa_cmp_pos, nsa_phi_w1, nsa_phi_b1, nsa_phi_w2, nsa_gate_b, fox_f_b,
              s5_lambda_re, s5_lambda_im, s5_log_dt, s5_b_re, s5_b_im, s5_c_re, s5_c_im,
              s5_d, s5_glu_w, s5_glu_b, mix_group_g, mix_w_out, mix_post_g,
              xa_pre_g, xa_mem_g, xa_w_q, xa_w_kv, xa_w_o, xa_post_g,
              ffn2_pre_g, ffn2_w_gate, ffn2_w_up, ffn2_w_down, ffn2_post_g):
    S = x.shape[1]
    rope_mla = _rope_tables(S, MLA_ROPE_DIM)
    rope_nsa = _rope_tables(S, HEAD_DIM)
    h = x
    for l in range(DEPTH):
        u = _rmsnorm(h, ffn1_pre_g[l])
        h = h + MACARON_WEIGHT * _rmsnorm(_swiglu(u, ffn1_w_gate[l], ffn1_w_up[l], ffn1_w_down[l]), ffn1_post_g[l])

        u = _rmsnorm(h, mix_pre_g[l])
        y = _token_mixing(u, mix_w_in[l], mla_q_norm_g[l], mla_w_uq[l], mla_kv_norm_g[l], mla_w_ukv[l],
                          nsa_cmp_pos[l], nsa_phi_w1[l], nsa_phi_b1[l], nsa_phi_w2[l], nsa_gate_b[l], fox_f_b[l],
                          s5_lambda_re[l], s5_lambda_im[l], s5_log_dt[l], s5_b_re[l], s5_b_im[l],
                          s5_c_re[l], s5_c_im[l], s5_d[l], s5_glu_w[l], s5_glu_b[l],
                          mix_group_g[l], mix_w_out[l], rope_mla, rope_nsa)
        h = h + _rmsnorm(y, mix_post_g[l])

        u = _rmsnorm(h, xa_pre_g[l])
        m = _rmsnorm(mem, xa_mem_g[l])
        h = h + _rmsnorm(_cross_attention(u, m, xa_w_q[l], xa_w_kv[l], xa_w_o[l]), xa_post_g[l])

        u = _rmsnorm(h, ffn2_pre_g[l])
        h = h + MACARON_WEIGHT * _rmsnorm(_swiglu(u, ffn2_w_gate[l], ffn2_w_up[l], ffn2_w_down[l]), ffn2_post_g[l])
    return h


_drawn_inputs = setup_inputs


def setup_inputs(seed=0):
    import zlib

    import numpy as np

    out = dict(_drawn_inputs(seed))
    spreads = {}
    factors = {'ffn1_pre_g': 3.184,
     'ffn1_post_g': 4.516,
     'mla_q_norm_g': 8.0,
     'mla_kv_norm_g': 4.786,
     'nsa_phi_b1': 5.798,
     'nsa_gate_b': 8.0,
     's5_lambda_re': 8.0,
     's5_glu_w': 3.79,
     's5_glu_b': 8.0,
     'mix_group_g': 3.373,
     'mix_post_g': 3.37,
     'xa_pre_g': 3.747,
     'xa_post_g': 3.625,
     'ffn2_pre_g': 5.849,
     'ffn2_post_g': 8.0}
    for name, (base, spread) in spreads.items():
        noise = np.random.default_rng([zlib.crc32(name.encode()), seed]).standard_normal(out[name].shape)
        drawn = base * np.exp(spread * noise) if base else spread * noise
        out[name] = jnp.asarray(drawn.astype(out[name].dtype))
    for name, factor in factors.items():
        out[name] = (out[name] * factor).astype(out[name].dtype)
    return out
```

```python
from contextlib import ExitStack

import numpy as np
import concourse.bass as bass
from concourse import mybir

F32 = mybir.dt.float32
F32R = mybir.dt.float32r
ALU = mybir.AluOpType
ACT = mybir.ActivationFunctionType
AX = mybir.AxisListType

DEPTH, S, D, F = 2, 256, 1024, 2816
P = 128
TT = S // P
KT = D // P
UC = 256
UNIT = KT * UC
FU = F // UC
H, HD = 4, 64
MLA_D, MLA_R, MLA_Q, MLA_KV = 96, 32, 192, 128
QK_T = 96
CMP_LEN, CMP_STRIDE = 32, 16
NC_CMP = (S - CMP_LEN) // CMP_STRIDE + 1
CMP_KT = CMP_LEN * HD // P
G5, C5, ST5 = 16, 16, 64
PAIRS = G5 // 2
C2 = 2 * C5
CH = 4
NCH = S // CH
EPS = 1e-6
NEG = -1e30
GELU_A, GELU_S = 0.044715, 0.7978845608028654

I_CQ, I_CKV, I_KPE, I_NQ = 0, 192, 320, 352
I_KC, I_VC, I_KSL, I_VSL, I_KW, I_VW, I_G = 608, 672, 736, 800, 864, 928, 992
I_FQ, I_FK, I_FV, I_FF, I_S5, I_END = 1004, 1260, 1516, 1772, 1776, 2032
IN_UNITS = [[(I_S5, I_END)], [(I_CQ, I_CKV)], [(I_CKV, I_NQ)], [(I_NQ, I_KC)], [(I_KC, I_KW)],
            [(I_KW, I_FQ), (I_FF, I_S5)], [(I_FQ, I_FK)], [(I_FK, I_FV)], [(I_FV, I_FF)]]
N_IN = len(IN_UNITS)
IN_W = [sum(b - a for a, b in u) for u in IN_UNITS]
M_PHI = N_IN + 1
KV_UNITS = [N_IN, *range(M_PHI + 4, M_PHI + 11)]
KV_BANK = [1, 1, 0, 1, 0, 1, 0, 1]
M_OUT = M_PHI + 11
M_Q = M_OUT + 4
M_O = M_Q + 4
N_MID = M_O + 4
SLOTS = 3
assert N_MID % SLOTS == 0
MID_N = N_MID // SLOTS
PHI_M = list(range(M_PHI, M_PHI + 4))
FFN_SLOTS = ((0, 1, 2, 0), (1, 2, 0, 1))


def mid_slot(m):
    return (m + 1) % SLOTS


def ffn_uses(f, s):
    return sum(n * (s == q) for n, q in zip((FU, FU, FU - 1, 1), FFN_SLOTS[f]))


SLOT_USES = [ffn_uses(0, s) + MID_N + ffn_uses(1, s) for s in range(SLOTS)]
SPLITS = [SLOT_USES[s] - sum(mid_slot(m) == s for m in PHI_M) for s in range(SLOTS)]
N_UNITS = 2 * 3 * FU + N_MID

_at = 0


def _cols(n):
    global _at
    _at += n
    return _at - n


C_FFN1, C_MIX, C_XA, C_MEM, C_FFN2, C_GRP = (_cols(KT) for _ in range(6))
C_GLUB, C_PHIB, C_QN, C_KVN = _cols(2), _cols(4), _cols(2), _cols(1)
C_LR, C_LI, C_LDT = (_cols(PAIRS) for _ in range(3))
C_POS, C_GB, C_FB = _cols(2 * CMP_KT), _cols(3 * H), _cols(H)
NCOL = _at
_at = 0
W_UQ, W_UKV, W_GLU, W_PHI2 = _cols(2 * H * MLA_D), _cols(H * 128), _cols(2 * 256), _cols(4 * HD)
W_BR, W_BI, W_CR, W_CI, W_D = (_cols(PAIRS * C2) for _ in range(5))
NMAT = _at
_at = 0
K_ID, K_ONE, K_TRI, K_MASK = (_cols(P) for _ in range(4))
K_CNEG, K_C01 = _cols(TT * NC_CMP), _cols(TT * NC_CMP)
K_NCC, K_NSS, K_MCC, K_MSS = _cols(TT * HD), _cols(TT * HD), _cols(TT * MLA_R), _cols(TT * MLA_R)
K_MJ, K_MQ, K_HALF = _cols(CH + 1), _cols(NCH), _cols(3)
NCONST = _at


def constants():
    k = np.zeros((P, NCONST), np.float32)
    p, c = np.arange(P)[:, None], np.arange(P)[None, :]
    k[:, K_ID:K_ID + P] = p == c
    k[:, K_ONE:K_ONE + P] = 1.0
    k[:, K_TRI:K_TRI + P] = p <= c
    k[:, K_MASK:K_MASK + P] = np.where(c <= p, 0.0, NEG)
    end = np.arange(NC_CMP) * CMP_STRIDE + CMP_LEN - 1

    def tokens(base, table):
        n = table.shape[1]
        for t in range(TT):
            k[:, base + t * n:base + (t + 1) * n] = table[t * P:(t + 1) * P]

    seen = np.arange(S)[:, None] >= end[None, :]
    tokens(K_CNEG, np.where(seen, 0.0, NEG))
    tokens(K_C01, seen.astype(np.float32))
    for cc, ss, dim in ((K_NCC, K_NSS, HD), (K_MCC, K_MSS, MLA_R)):
        inv = np.float32(1.0) / (np.float32(10000.0) ** (np.arange(0, dim, 2, dtype=np.float32) / np.float32(dim)))
        ang = np.arange(S, dtype=np.float32)[:, None] * inv[None, :].astype(np.float32)
        tokens(cc, np.tile(np.cos(ang), (1, 2)))
        tokens(ss, np.tile(np.sin(ang), (1, 2)))
    k[:, K_MJ:K_MJ + CH + 1] = np.arange(CH + 1)
    k[:, K_MQ:K_MQ + NCH] = np.arange(NCH)
    k[:, K_HALF:K_HALF + 1] = -0.5
    k[:, K_HALF + 1:K_HALF + 2] = -1.0
    k[:, K_HALF + 2:K_HALF + 3] = np.pi / 2
    return k


def program(nc, x, memory, weights, cols, mats, post, consts, out, mem_scratch):
    ctx = ExitStack()
    with ctx:
        def sb(name, n, dt=F32):
            return ctx.enter_context(nc.sbuf_tensor(name, [P, n], dt))

        raw = [sb(f"raw{s}", UNIT) for s in range(SLOTS)]
        w_hi = [sb(f"w_hi{s}", UNIT, F32R) for s in range(SLOTS)]
        w_lo = [sb(f"w_lo{s}", UNIT, F32R) for s in range(SLOTS)]
        x_hi = sb("x_hi", KT * S, F32R)
        x_lo = sb("x_lo", KT * S, F32R)
        hid_hi = sb("hid_hi", 2 * S, F32R)
        hid_lo = sb("hid_lo", 2 * S, F32R)
        h = sb("h", TT * D)
        work = sb("work", TT * D)
        gain = sb("gain", D)
        pcol = sb("pcol", NCOL)
        pmat = sb("pmat", NMAT)
        con = sb("con", NCONST)
        proj = sb("proj", TT * I_FV)
        mix_out = sb("mix_out", TT * 3 * 256)
        v_mla = sb("v_mla", TT * H * 65)
        v_fox = sb("v_fox", TT * H * 65)
        v_nsa = sb("v_nsa", 2 * TT * 65)
        qk_a = sb("qk_a", 2 * H * S)
        nsa_q = sb("nsa_q", H * S)
        nsa_k = sb("nsa_k", 2 * S)
        kc2 = sb("kc2", 2 * S)
        zone = sb("zone", 8192)
        rope_t = sb("rope_t", 1024)
        st = sb("st", 160)
        small = sb("small", 576)

        PS = ctx.enter_context(nc.psum_tensor("PS", [P, 8 * 512], F32))

        def bank(b, n=1):
            return PS[:, b * 512:(b + n) * 512]

        def v3(ap_, how_, **kw):
            return ap_.rearrange(how_, **kw)

        ident = con[:, K_ID:K_ID + P]
        ones = con[:, K_ONE:K_ONE + P]
        tri = con[:, K_TRI:K_TRI + P]
        mask = con[:, K_MASK:K_MASK + P]
        h3 = v3(h[:, :], "p (t d) -> p t d", t=TT)
        w3 = v3(work[:, :], "p (t d) -> p t d", t=TT)
        xh3 = v3(x_hi[:, :], "p (k s) -> p k s", k=KT)
        xl3 = v3(x_lo[:, :], "p (k s) -> p k s", k=KT)
        y_sq_rows = [mix_out[:, 0:D], proj[:, 0:D]]
        pr3 = v3(proj[:, :], "p (t n) -> p t n", t=TT)
        mo = v3(mix_out[:, :], "p (t m h d) -> p t m h d", t=TT, m=3, h=H)
        q_tok = v3(mix_out[:, 0:TT * 384], "p (t h d) -> p t h d", t=TT, h=H)
        k_tok = v3(mix_out[:, TT * 384:TT * 768], "p (t h d) -> p t h d", t=TT, h=H)
        vm = v3(v_mla[:, :], "p (t h d) -> p t h d", t=TT, h=H)
        vf = v3(v_fox[:, :], "p (t h d) -> p t h d", t=TT, h=H)
        vn = v3(v_nsa[:, :], "p (b t d) -> p b t d", b=2, t=TT)
        qa = v3(qk_a[:, 0:H * S], "p (h s) -> p h s", h=H)
        ka = v3(qk_a[:, H * S:2 * H * S], "p (h s) -> p h s", h=H)
        qn = v3(nsa_q[:, :], "p (h s) -> p h s", h=H)
        kn = v3(nsa_k[:, :], "p (b s) -> p b s", b=2)
        kc = v3(kc2[:, :], "p (j s) -> p j s", j=2)
        bl = v3(zone[:, 7696:8176], "p (j k n) -> p j k n", j=2, k=CMP_KT)
        f_th, f_t, f_hid = work[:, 0:512], work[:, 512:1024], work[:, 1024:1536]
        s_w = [v3(qk_a[:, i * 1024:(i + 1) * 1024], "p (g j c) -> p g j c", g=PAIRS, j=CH) for i in range(2)]
        s_lb = v3(zone[:, 0:2048], "p (i g n) -> p i g n", i=2, g=PAIRS)
        s_b4 = [v3(zone[:, i * 1024:(i + 1) * 1024], "p (g n) -> p g n", g=PAIRS) for i in range(2)]
        s_t0 = v3(zone[:, 2048:3072], "p (g r c) -> p g r c", g=PAIRS, r=CH)
        s_cs = [v3(zone[:, 3072 + i * 512:3584 + i * 512], "p (g q) -> p g q", g=PAIRS) for i in range(2)]
        s_c = [v3(zone[:, 4096 + i * 1280:5376 + i * 1280], "p (g j c) -> p g j c", g=PAIRS, j=CH + 1)
               for i in range(2)]
        s_x = [v3(zone[:, 6656 + i * 520:7176 + i * 520], "p (g q) -> p g q", g=PAIRS) for i in range(2)]
        s_u = v3(rope_t[:, 0:512], "p (g q) -> p g q", g=PAIRS)
        s_tmp = [work[:, i * 512:(i + 1) * 512] for i in range(4)]
        s_out = v3(work[:, 1536:2048], "p (i s) -> p i s", i=2)
        xk = v3(zone[:, 0:2048], "p (k s) -> p k s", k=KT)
        xv = v3(zone[:, 2048:4096], "p (t d) -> p t d", t=TT)
        probs = zone[:, 4096:5632]
        probs_t = zone[:, 5632:7168]
        xq = v3(proj[:, 0:2048], "p (k s) -> p k s", k=KT)

        s_yt = v3(work[:, 0:512], "p (i s) -> p i s", i=2)
        s_mag = v3(kc2[:, :], "p (g q) -> p g q", g=PAIRS)
        cq_t = v3(nsa_q[:, 0:512], "p (k s) -> p k s", k=2)
        ckv_t = nsa_q[:, 512:768]
        lf = v3(rope_t[:, 768:768 + TT * P], "p (t c) -> p t c", t=TT)
        ncum = zone[:, 7168:7424]
        rows_of_t = v3(PS[:, 4 * 512:], "p (k s) -> p k s", k=KT)
        y_ps = v3(PS[:, 0:4 * 512], "p (t d) -> p t d", t=TT)

        _s = [0]

        def sm(n):
            _s[0] += n
            assert _s[0] <= 576
            return small[:, _s[0] - n:_s[0]]

        dt_, lrdt, th, kk8, tt8, r4 = (sm(8) for _ in range(6))
        magj, csj, snj, arj, aij, narj, naij, laj = (sm(40) for _ in range(8))
        krd, kid, t8a, t8b, den, rden = (sm(8) for _ in range(6))
        half_b = sm(2)
        flog = v3(sm(8), "p (t h) -> p t h", t=TT)
        gates = v3(sm(24), "p (t b h) -> p t b h", t=TT, b=3)
        hx, hx2 = sm(60), sm(60)
        _t = [0]

        def stat(n):
            _t[0] += n
            assert _t[0] <= 160
            return st[:, _t[0] - n:_t[0]]

        NORMS = 10
        N_PF1, N_QF1, N_PM, N_MLA, N_GRP, N_QM, N_PX, N_QX, N_PF2, N_QF2 = range(NORMS)
        norm_w = [2] * NORMS
        RSTD = (0, 2, 4, 6, 7, 8, 10, 12, 14, 16)
        norm_w[N_MLA], norm_w[N_GRP] = 4, 6
        ss = [stat(w) for w in norm_w]
        rstd = [stat(w) for w in norm_w]
        mx, nb, rc, cumt = (stat(8) for _ in range(4))
        s5_r = stat(TT)
        f_a, f_b2 = v3(stat(8), "p (t h) -> p t h", t=TT), v3(stat(8), "p (t h) -> p t h", t=TT)
        kct, vct = rope_t[:, 0:16], rope_t[:, 16:80]
        cp = v3(rope_t[:, 128:128 + 120], "p (a n) -> p a n", n=NC_CMP)
        cq8, cs8 = rope_t[:, 256:264], rope_t[:, 264:272]

        sem, growth = {}, {}

        def signal(name, per_layer):
            sem[name], growth[name] = ctx.enter_context(nc.semaphore(name)), per_layer
            return name

        def bc(ap, dim, n):
            a = ap.unsqueeze(dim)
            return a.to_broadcast([n if i == dim else d for i, d in enumerate(a.shape)])

        raw_in = [signal(f"raw_in{s}", 16 * SLOT_USES[s]) for s in range(SLOTS)]
        hi_done = [signal(f"hi_done{s}", SPLITS[s]) for s in range(SLOTS)]
        split_done = [signal(f"split_done{s}", SPLITS[s]) for s in range(SLOTS)]
        unit_done = [signal(f"unit_done{s}", SLOT_USES[s]) for s in range(SLOTS)]
        for name, n in dict(
                pcol_in=16, pmat_in=16, gain_in=64, mem_in=16,
                y_half=4, y_sq=8, h_sq=8, mla_sq=1, grp_sq=1, var_done=2, rstd_done=18, xn_ready=8, xt_ready=16,
                x_hi_done=52, x_split=52, h_done=8,
                tanh_done=2 * FU, gated=2 * FU, hid_done=2 * FU, hid_hi_done=2 * FU, hid_split=2 * FU,
                dt_done=1, expo_ready=1, ang_ready=1, trig_done=1, s5_c_done=1, s5_w_done=1,
                proj_done=N_IN, s5_u_dve=1, s5_t=1, s5_lb_act=1, s5_lb_dve=1, s5_k=1, s5_kd=1,
                s5_t0_act=1, s5_t0_dve=1, s5_v=1, s5_x=1, s5_y=1, s5_yc=1, s5_ga=1, s5_th=1, s5_g=1,
                s5_sc_act=1, s5_sc_dve=1, s5_z=1, s5_zt=1, s5_sq=1, s5_ss=1, s5_var=1, s5_rstd=1, s5_rstd_all=1, s5_out=1,
                mla_xn=1, mla_t1=1, mla_t1c=1, mla_qkv=1, mla_nope=1, mla_tok=1, mla_t2=1, mla_qt=1, mla_kt=1,
                nsa_rope=1, nsa_v=1, nsa_t=1, nsa_kc=1, nsa_tc_act=1, nsa_tc_dve=1, blocks_done=1,
                phi_x=1, phi_th=1, phi_hid=1, phi_out=1, phi_c=1,
                gate_x=1, gate_th=1, gates_done=1,
                cmp_s=1, cmp_x=1, cmp_e=1, cmp_p=1, cmp_t=1, cmp_tc=1, cmp_o=1, cmp_done=1,
                fox_x=1, fox_e=1, fox_ln=1, fox_lf=1, fox_cum=1, fox_nc=1, fox_ct=1,
                fox_tq=1, fox_tk=1, fox_qt=1, fox_kt=1,
                att_s=4, att_max=4, att_exp=4, att_t=4, att_tc_act=4, att_tc_dve=4, att_pv=4, att_out=4,
                grp_xn=1, grp_t=3, xkv_done=8, xq_done=4, xs=4, xmax=4, xexp=4, xp=4, xt=4, xtc=4, xo=4, xoc=4,
        ).items():
            signal(name, n)
        CREDIT = {"h_done", "hid_done", *unit_done, *split_done}
        own = {e: ctx.enter_context(nc.semaphore(f"{e}_order")) for e in ("act", "dve", "pool")}
        own_steps = {"act": 1, "dve": 65, "pool": 88}
        pool_held = ctx.enter_context(nc.semaphore("pool_held"))
        s_con = ctx.enter_context(nc.semaphore("con_in"))
        x_in = ctx.enter_context(nc.semaphore("x_in"))
        s_mem = ctx.enter_context(nc.semaphore("mem_rows_in"))
        s_memst = ctx.enter_context(nc.semaphore("mem_scratch_out"))
        s_first = ctx.enter_context(nc.semaphore("first_params_in"))
        out_stored = ctx.enter_context(nc.semaphore("out_stored"))
        b_one, b_ss, b_var, b_rstd, b_xn, b_t, b_tc = (ctx.enter_context(nc.semaphore(n)) for n in (
            "start_ones", "start_ss", "start_var", "start_rstd", "start_xn", "start_t", "start_tc"))

        class Engine:

            def __init__(self, eng, name, l):
                self.e, self.name, self.l, self.k = eng, name, l, 0

            def at(self, name, n):
                return sem[name], self.l * growth[name] + n + (name in CREDIT)

            def step(self, ins):
                ins.then_inc(own[self.name], 1)
                self.k += 1
                self.e.wait_ge(own[self.name], self.l * own_steps[self.name] + self.k)
                if self.name == "pool":
                    self.e.sem_inc(pool_held)

            def end(self):
                assert self.name not in own_steps or self.k == own_steps[self.name], (self.name, self.k)

        def mid(m):
            s = mid_slot(m)
            n = ffn_uses(0, s) + sum(mid_slot(q) == s for q in range(m))
            return s, n, n - sum(mid_slot(q) == s and q < m for q in PHI_M)

        def ffn_base(f):
            at = [(s, f * (ffn_uses(0, s) + MID_N), f * (SPLITS[s] - ffn_uses(1, s))) for s in FFN_SLOTS[f]]
            (g, n, ns) = at[0]
            return [*at[:3], (g, n + FU, ns + FU)]

        FILL = [0, 8, 16, 24, 32, 40, 44]
        FI_F1, FI_MIX, FI_MEM, FI_MO, FI_XA, FI_XO, FI_F2 = range(7)
        MO_ORDER = [6, 7, 0, 1, 2, 3, 4, 5]
        PRE = [(N_PF1, FI_F1, C_FFN1), (N_PM, FI_MIX, C_MIX), (N_PX, FI_XA, C_XA), (N_PF2, FI_F2, C_FFN2)]
        POST = [N_QF1, N_QM, N_QX, N_QF2]
        Y_DONE = [(unit_done[s_], n_ + 1) for s_, n_, _ in (ffn_base(0)[3], mid(M_OUT + 3), mid(M_O + 3), ffn_base(1)[3])]
        SCALE = {0: MLA_D ** -0.5, 1: HD ** -0.5, 2: HD ** -0.5, 3: HD ** -0.5}
        POS = (0, 2, 3, 1)
        HALO = (MLA_D, HD, HD, HD)

        def head_q(g, hh):
            return (qn if g in (1, 2) else qa)[0:HALO[g], hh]

        def head_k(g, hh):
            return kn[0:HD, g - 1] if g in (1, 2) else ka[0:HALO[g], hh]

        def head_v(g, t, hh):
            return vn[:, g - 1, t] if g in (1, 2) else (vm if g == 0 else vf)[:, t, hh]

        s1 = v3(bank(2, 2), "p (h s) -> p h s", h=H)
        s0 = v3(bank(4), "p (h s) -> p h s", h=H)
        o_ps = [v3(bank(b)[:, 0:H * 65], "p (h d) -> p h d", h=H) for b in (4, 2)]
        k_ps = v3(bank(2, 2), "p (g n) -> p g n", g=PAIRS)
        c_ps = v3(bank(5)[:, 128:256], "p (a n) -> p a n", n=16)
        x_f = v3(x_hi[:, :].bitcast(F32), "p (k s) -> p k s", k=KT)
        hid_f = hid_hi[:, :].bitcast(F32)
        w_f = [w[:, :].bitcast(F32) for w in w_hi]

        block = ctx.enter_context(nc.Block())

        @block.sync
        def _(sp):
            sp.dma_start(con[:, :], consts).then_inc(s_con, 16)
            sp.dma_start(work[:, :].rearrange("p (t d) -> p t d", t=TT),
                         memory.rearrange("(t p) d -> p t d", p=P)).then_inc(s_mem, 16)
            sp.dma_start(h3, x.rearrange("(t p) d -> p t d", p=P)).then_inc(x_in, 16)
            sp.dma_start(pcol[:, :], cols[0]).then_inc(s_first, 16)
            sp.dma_start(pmat[:, :], mats[0]).then_inc(s_first, 16)
            with sp.Fori(0, DEPTH) as l:
                E = Engine(sp, "sp", l)

                def load(s, unit):
                    sp.dma_start(raw[s][:, :], weights[l * N_UNITS + unit]).then_inc(sem[raw_in[s]], 16)

                def ffn_loads(f):
                    base = f * (3 * FU + N_MID)
                    (g_, _, g0), (u_, _, u0), (d_, _, d0), (z_, _, z0) = ffn_base(f)
                    sp.wait_ge(*E.at(split_done[g_], g0))
                    load(g_, base)
                    sp.wait_ge(*E.at(split_done[u_], u0))
                    load(u_, base + 1)
                    with sp.Fori(1, FU) as i:
                        sp.wait_ge(*E.at(split_done[g_], g0 + i))
                        load(g_, base + i * 3 - 1)
                        sp.wait_ge(*E.at(split_done[u_], u0 + i))
                        load(u_, base + i * 3)
                        sp.wait_ge(*E.at(split_done[d_], d0 - 1 + i))
                        load(d_, base + i * 3 + 1)
                    sp.wait_ge(*E.at(split_done[z_], z0))
                    load(z_, base + 3 * FU - 1)

                ffn_loads(0)
                for m in range(N_MID):
                    s, n, ns = mid(m)
                    if m - SLOTS in PHI_M:
                        sp.wait_ge(*E.at(unit_done[s], n))
                    else:
                        sp.wait_ge(*E.at(split_done[s], ns))
                    load(s, 3 * FU + m)
                ffn_loads(1)

        @block.gpsimd
        def _(pool):
            g = nc.gpsimd
            for name in sorted(CREDIT):
                pool.sem_inc(sem[name], 1)
            pool.memset(v3(v_mla[:, :], "p (n d) -> p n d", d=65)[:, :, 64:65], 1.0)
            pool.memset(v3(v_fox[:, :], "p (n d) -> p n d", d=65)[:, :, 64:65], 1.0)
            pool.memset(v3(v_nsa[:, :], "p (n d) -> p n d", d=65)[:, :, 64:65], 1.0).then_inc(b_one, 1)
            pool.wait_ge(s_con, 16)
            half = con[:, K_HALF:K_HALF + 1]
            minus1 = con[:, K_HALF + 1:K_HALF + 2]
            pool.wait_ge(b_var, 1)
            g.tensor_tensor(rstd[0], ss[0], half.to_broadcast([P, 2]), ALU.pow).then_inc(b_rstd, 1)
            with pool.Fori(0, DEPTH) as l:
                E = Engine(pool, "pool", l)

                def row_rstd(n, name, at):
                    for t in range(TT):
                        pool.wait_ge(*E.at(name, at + t + 1))
                        pool.sem_inc(pool_held)
                        c_ = slice(t, t + 1)
                        ts(ss[n][:, c_], ss[n][:, c_], EPS, ALU.add)
                        g.tensor_tensor(rstd[n][:, c_], ss[n][:, c_], half, ALU.pow).then_inc(sem["rstd_done"], 1)

                def norm_rstd(n, k):
                    pool.wait_ge(*E.at("var_done", k + 1))
                    pool.sem_inc(pool_held)
                    g.tensor_tensor(rstd[n], ss[n], half.to_broadcast([P, norm_w[n]]), ALU.pow).then_inc(sem["rstd_done"], 1)

                def tt(o, a, b, op):
                    E.step(g.tensor_tensor(o, a, b, op))

                def ts(o, a, s1, op0, s2=None, op1=ALU.bypass):
                    E.step(g.tensor_scalar(o, a, s1, s2, op0, op1))

                def reduce_angle(a, k, t):
                    ts(k, a, 0.15915494309189535, ALU.mult)
                    ts(k, k, 12582912.0, ALU.add)
                    ts(k, k, 12582912.0, ALU.subtract)
                    for part in (6.28125, 1.9350051879882812e-3, 3.0199159819567e-7):
                        ts(t, k, part, ALU.mult)
                        tt(a, a, t, ALU.subtract)

                row_rstd(N_PF1, "h_sq", 0)
                LR, LI = pcol[:, C_LR:C_LR + PAIRS], pcol[:, C_LI:C_LI + PAIRS]
                pool.wait_ge(*E.at("dt_done", 1))
                pool.sem_inc(pool_held)
                tt(lrdt, LR, dt_, ALU.mult)
                tt(th, LI, dt_, ALU.mult)
                powers = con[:, K_MJ:K_MJ + CH + 1]

                def gj(a, w=CH + 1):
                    return v3(a, "p (g j) -> p g j", j=w)

                g.tensor_tensor(gj(laj), bc(lrdt, 2, CH + 1), bc(powers, 1, PAIRS), ALU.mult).then_inc(sem["expo_ready"], 1)
                reduce_angle(th, kk8, tt8)
                ts(r4, th, float(CH), ALU.mult)
                reduce_angle(r4, kk8, tt8)
                ang, cang = nsa_q[:, 0:552], proj[:, 0:552]
                tt(gj(ang[:, 0:40]), bc(th, 2, CH + 1), bc(powers, 1, PAIRS), ALU.mult)
                tt(gj(ang[:, 40:552], NCH), bc(r4, 2, NCH), bc(con[:, K_MQ:K_MQ + NCH], 1, PAIRS), ALU.mult)
                reduce_angle(ang, cang, proj[:, 600:1152])
                g.tensor_scalar(ang, ang, 3.1415925, -3.1415925, ALU.min, ALU.max).then_inc(sem["ang_ready"], 1)
                pool.wait_ge(*E.at("trig_done", 1))
                pool.sem_inc(pool_held)
                tt(arj, magj, csj, ALU.mult)
                tt(aij, magj, snj, ALU.mult)
                ts(narj, arj, -1.0, ALU.mult)
                ts(naij, aij, -1.0, ALU.mult)
                q01 = kc2[:, 0:NCH]
                ts(r4, gj(magj)[:, :, CH:CH + 1], 1.0, ALU.mult)
                ts(q01, con[:, K_MQ:K_MQ + NCH], 1.0, ALU.min)
                ar1, ai1 = gj(arj)[:, :, 1:2], gj(aij)[:, :, 1:2]
                cr8 = v3(kk8, "p (g o) -> p g o", o=1)
                e3 = [v3(a, "p (g o) -> p g o", o=1) for a in (krd, kid, t8a, t8b, den, rden, LR, LI)]
                kr_, ki_, ta, tb, de, rd, lr_, li_ = e3
                ts(cr8, ar1, -1.0, ALU.add)
                tt(ta, lr_, lr_, ALU.mult)
                tt(tb, li_, li_, ALU.mult)
                tt(de, ta, tb, ALU.add)
                tt(rden, den, minus1.to_broadcast([P, PAIRS]), ALU.pow)
                tt(ta, cr8, lr_, ALU.mult)
                tt(tb, ai1, li_, ALU.mult)
                tt(ta, ta, tb, ALU.add)
                tt(kr_, ta, rd, ALU.mult)
                tt(ta, ai1, lr_, ALU.mult)
                tt(tb, cr8, li_, ALU.mult)
                tt(ta, ta, tb, ALU.subtract)
                tt(ki_, ta, rd, ALU.mult)

                def m3(at):
                    return v3(pmat[:, at:at + PAIRS * C2], "p (g c) -> p g c", g=PAIRS)

                def over_c(a, w, n):
                    return bc(gj(a)[:, :, 0:w], 3, C2)

                J5 = CH + 1
                tc5 = v3(proj[:, 0:1280], "p (g j c) -> p g j c", g=PAIRS, j=J5)
                crw, ciw = bc(m3(W_CR), 2, J5), bc(m3(W_CI), 2, J5)
                tt(s_c[0], crw, over_c(arj, J5, 0), ALU.mult)
                tt(tc5, ciw, over_c(aij, J5, 0), ALU.mult)
                tt(s_c[0], s_c[0], tc5, ALU.subtract)
                tt(s_c[1], crw, over_c(naij, J5, 0), ALU.mult)
                tt(tc5, ciw, over_c(narj, J5, 0), ALU.mult)
                g.tensor_tensor(s_c[1], s_c[1], tc5, ALU.add).then_inc(sem["s5_c_done"], 1)
                br, bi, tb1, tb2 = m3(W_BR), m3(W_BI), v3(nsa_q[:, 0:256], "p (g c) -> p g c", g=PAIRS), \
                    v3(nsa_q[:, 256:512], "p (g c) -> p g c", g=PAIRS)
                tb3 = v3(nsa_q[:, 512:768], "p (g c) -> p g c", g=PAIRS)
                krw, kiw = bc(krd, 2, C2), bc(kid, 2, C2)
                tt(tb1, br, krw, ALU.mult)
                tt(tb2, bi, kiw, ALU.mult)
                tt(tb1, tb1, tb2, ALU.subtract)
                tt(tb2, bi, krw, ALU.mult)
                tt(tb3, br, kiw, ALU.mult)
                tt(tb2, tb2, tb3, ALU.add)
                brw, biw = bc(tb1, 2, CH), bc(tb2, 2, CH)
                tw = v3(proj[:, 1280:2304], "p (g j c) -> p g j c", g=PAIRS, j=CH)
                tt(s_w[0], brw, over_c(arj, CH, 0), ALU.mult)
                tt(tw, biw, over_c(aij, CH, 0), ALU.mult)
                tt(s_w[0], s_w[0], tw, ALU.subtract)
                tt(s_w[1], brw, over_c(aij, CH, 0), ALU.mult)
                tt(tw, biw, over_c(arj, CH, 0), ALU.mult)
                tt(s_w[1], s_w[1], tw, ALU.add)
                for q, src in enumerate((brw, biw)):
                    ts(v3(zone[:, q * 1024:(q + 1) * 1024], "p (g j c) -> p g j c", g=PAIRS, j=CH), src, 1.0, ALU.mult)
                ts(v3(rope_t[:, 0:NCH], "p (g q) -> p g q", g=1), v3(q01, "p (g q) -> p g q", g=1), 1.0, ALU.mult)
                tt(s_mag, bc(r4, 2, NCH), bc(rope_t[:, 0:NCH], 1, PAIRS), ALU.mult)
                pool.memset(s_x[0][:, :, 0:1], 0.0)
                pool.memset(s_x[1][:, :, 0:1], 0.0)
                pool.memset(s_t0, 0.0).then_inc(sem["s5_w_done"], 1)
                row_rstd(N_QF1, "y_sq", 0)
                row_rstd(N_PM, "h_sq", 2)
                norm_rstd(N_MLA, 0)
                pool.wait_ge(*E.at("proj_done", 6))
                pool.sem_inc(pool_held)
                pool.tensor_copy(vn[:, 0, :, 0:HD], pr3[:, :, I_VSL:I_VSL + HD])
                pool.tensor_copy(vn[:, 1, :, 0:HD], pr3[:, :, I_VW:I_VW + HD]).then_inc(sem["nsa_v"], 1)
                pool.wait_ge(*E.at("s5_var", 1))
                pool.sem_inc(pool_held)
                g.tensor_tensor(s5_r, s5_r, half.to_broadcast([P, TT]), ALU.pow).then_inc(sem["s5_rstd"], 1)
                norm_rstd(N_GRP, 1)
                row_rstd(N_QM, "y_sq", 2)
                row_rstd(N_PX, "h_sq", 4)
                row_rstd(N_QX, "y_sq", 4)
                row_rstd(N_PF2, "h_sq", 6)
                row_rstd(N_QF2, "y_sq", 6)
                E.end()

        @block.scalar
        def _(act):
            a = nc.scalar
            act.wait_ge(s_mem, 16)
            for t in range(TT):
                i = a.activation(zone[:, t * D:(t + 1) * D], w3[:, t], ACT.Square, accum_out=ss[0][:, t:t + 1])
            i.then_inc(b_ss, 1)
            act.wait_ge(b_t, 1)
            a.activation(zone[:, 0:2048], PS[:, 4 * 512:8 * 512], ACT.Copy).then_inc(b_tc, 1)
            act.wait_ge(b_tc, 1)
            act.dma_start(mem_scratch, zone[:, 0:2048]).then_inc(s_memst, 16)
            act.wait_ge(x_in, 16)
            act.wait_ge(s_first, 32)
            act.wait_ge(s_memst, 16)
            with act.Fori(0, DEPTH) as l:
                E = Engine(act, "act", l)

                def split(s, n, ns, w=UC):
                    act.wait_ge(*E.at(unit_done[s], n))
                    act.wait_ge(*E.at(raw_in[s], n * 16 + 16))
                    o, i = (v3(x_[:, :], "p (k n) -> p k n", n=UC)[:, :, 0:w] for x_ in (w_hi[s], raw[s]))
                    a.activation(o, i, ACT.Copy).then_inc(sem[hi_done[s]], 1)

                def split_mid(m):
                    s, n, ns = mid(m)
                    split(s, n, ns, IN_W[m] if m < N_IN else UC)

                def y_squares(q):
                    for t in range(TT):
                        if t == 0:
                            act.wait_ge(*E.at("y_half", q + 1))
                        else:
                            act.wait_ge(*E.at(*Y_DONE[q]))
                        if q == 0 and t == 1:
                            act.wait_ge(*E.at("s5_w_done", 1))
                        a.activation(y_sq_rows[t], y_ps[:, t], ACT.Square, scale=D ** -0.5,
                                     accum_out=ss[POST[q]][:, t:t + 1]).then_inc(sem["y_sq"], 1)

                def h_squares(p):
                    for t in range(TT):
                        act.wait_ge(*E.at("h_done", 2 * p - (TT - 1 - t) if p else 0))
                        a.activation(w3[:, t], h3[:, t], ACT.Square, scale=D ** -0.5,
                                     accum_out=ss[PRE[p][0]][:, t:t + 1]).then_inc(sem["h_sq"], 1)

                def fill_hi(p):
                    n, fi, gc = PRE[p]
                    for k in range(KT):
                        if k % 2 == 0:
                            act.wait_ge(*E.at("xt_ready", 4 * p + k // 2 + 1))
                        a.activation(xh3[:, k], rows_of_t[:, k], ACT.Copy, scale=pcol[:, gc + k:gc + k + 1]).then_inc(sem["x_hi_done"], 1)

                def ffn_piece(f, i, last):
                    (g_, g, gs), (u_, u, us), (d_, d, ds), _ = ffn_base(f)
                    if not isinstance(i, int) or i > 0:
                        split(d_, d - 1 + i, ds - 1 + i)
                        act.wait_ge(*E.at(unit_done[d_], d - 1 + i))
                        act.wait_ge(*E.at("hid_done", f * FU + i))
                        a.activation(hid_hi[:, :], f_hid, ACT.Copy).then_inc(sem["hid_hi_done"], 1)
                    if not last:
                        split(g_, g + 1 + i, gs + 1 + i)
                    act.wait_ge(*E.at(unit_done[g_], g + 1 + i))
                    a.activation(f_th, bank(4), ACT.Tanh, scale=0.5).then_inc(sem["tanh_done"], 1)
                    if not last:
                        split(u_, u + 1 + i, us + 1 + i)

                def ffn_tail(f):
                    _, _, (d_, d, _), (z_, z, zs) = ffn_base(f)
                    split(z_, z, zs)
                    act.wait_ge(*E.at(unit_done[d_], d + FU - 1))
                    act.wait_ge(*E.at("hid_done", f * FU + FU))
                    a.activation(hid_hi[:, :], f_hid, ACT.Copy).then_inc(sem["hid_hi_done"], 1)

                def load_gain(n):
                    act.wait_ge(*E.at("h_done", 2 * n))
                    act.dma_start(gain[:, :], post[l * 4 + n].unsqueeze(0).to_broadcast([P, D])) \
                       .then_inc(sem["gain_in"], 16)

                h_squares(0)
                split(0, 0, 0)
                fill_hi(0)
                split(1, 0, 0)
                load_gain(0)
                a.activation(dt_, pcol[:, C_LDT:C_LDT + PAIRS], ACT.Exp).then_inc(sem["dt_done"], 1)
                ffn_piece(0, 0, False)
                with act.Fori(1, FU // 2) as i:
                    ffn_piece(0, i, False)
                    act.wait_ge(s_con, 16)
                act.wait_ge(*E.at("expo_ready", 1))
                a.activation(magj, laj, ACT.Exp)
                act.wait_ge(*E.at("ang_ready", 1))
                E.step(a.activation(proj[:, 0:552], nsa_q[:, 0:552], ACT.Abs))
                quarter = con[:, K_HALF + 2:K_HALF + 3]
                a.activation(snj, nsa_q[:, 0:40], ACT.Sin)
                a.activation(csj, proj[:, 0:40], ACT.Sin, scale=-1.0, bias=quarter)
                a.activation(zone[:, 3072:3584], proj[:, 40:552], ACT.Sin, scale=-1.0, bias=quarter)
                a.activation(zone[:, 3584:4096], nsa_q[:, 40:552], ACT.Sin).then_inc(sem["trig_done"], 1)
                with act.Fori(FU // 2, FU - 1) as i:
                    ffn_piece(0, i, False)
                    act.wait_ge(s_con, 16)
                ffn_piece(0, FU - 1, True)
                ffn_tail(0)
                split_mid(0)
                split_mid(1)
                y_squares(0)
                h_squares(1)
                fill_hi(1)
                load_gain(1)

                def evac(m):
                    s, n, _ = mid(m)
                    act.wait_ge(*E.at(unit_done[s], n + 1))
                    src = v3(bank(m % 2), "p (t n) -> p t n", t=TT)
                    if m == 5:
                        a.activation(pr3[:, :, I_KW:I_FQ], src[:, :, 0:I_FQ - I_KW], ACT.Copy)
                        i = a.activation(flog, src[:, :, I_FQ - I_KW:I_FQ - I_KW + H], ACT.Copy)
                    elif m == 8:
                        i = a.activation(vf[:, :, :, 0:HD], v3(bank(m % 2), "p (t h d) -> p t h d", t=TT, h=H),
                                         ACT.Copy)
                    else:
                        (lo, hi), = IN_UNITS[m]
                        i = a.activation(pr3[:, :, lo:hi], src[:, :, 0:hi - lo], ACT.Copy)
                    i.then_inc(sem["proj_done"], 1)

                split_mid(2)
                s, n, _ = mid(0)
                act.wait_ge(*E.at(unit_done[s], n + 1))
                act.wait_ge(*E.at("s5_w_done", 1))
                u_ps = v3(bank(0), "p (i q r) -> p i q r", i=2, r=CH)
                u_to = v3(s_u.rearrange("p g q -> p (g q)"), "p (i a q) -> p a i q", i=2, a=4)
                for j in range(2):
                    for q in range(4):
                        i = a.activation(u_to[32 * j:32 * j + 32, q], u_ps[32 * q:32 * q + 32, :, :, CH - 1 - j],
                                         ACT.Copy)
                i.then_inc(sem["proj_done"], 1)
                split_mid(3)
                evac(1)
                split_mid(4)
                evac(2)
                act.wait_ge(*E.at("proj_done", 3))
                for q, (lo, w) in enumerate(((I_CQ, MLA_Q), (I_CKV, MLA_KV))):
                    for t in range(TT):
                        at = q * 2 * MLA_Q + t * w
                        i = a.activation(nsa_q[:, at:at + w], pr3[:, t, lo:lo + w], ACT.Square,
                                         accum_out=ss[N_MLA][:, 2 * q + t:2 * q + t + 1])
                i.then_inc(sem["mla_sq"], 1)
                act.wait_ge(*E.at("s5_t", 1))
                act.wait_ge(*E.at("s5_k", 1))
                a.activation(zone[:, 0:1024], bank(4, 2),
                                 ACT.Copy).then_inc(sem["s5_lb_act"], 1)
                split_mid(5)
                evac(3)
                act.wait_ge(*E.at("s5_kd", 1))
                for j in (2, 3):
                    i = a.activation(s_t0[32 * j:32 * j + 32, :, CH - 1 - j:CH, :],
                                     v3(bank(2, 2), "p (g r c) -> p g r c", g=PAIRS, r=CH)
                                     [32 * j:32 * j + 32, :, 0:j + 1, :], ACT.Copy)
                i.then_inc(sem["s5_t0_act"], 1)
                act.wait_ge(*E.at("mla_t1", 1))
                for k in range(2):
                    a.activation(cq_t[0:QK_T, k], bank(6)[0:QK_T, k * S:(k + 1) * S], ACT.Copy,
                                 scale=pcol[0:QK_T, C_QN + k:C_QN + k + 1])
                a.activation(ckv_t, bank(7)[:, 0:S], ACT.Copy, scale=pcol[:, C_KVN:C_KVN + 1]).then_inc(sem["mla_t1c"], 1)
                split_mid(6)
                evac(4)
                act.wait_ge(*E.at("mla_qkv", 1))
                qp = v3(bank(2, 2), "p (t n) -> p t n", t=TT)[:, :, 0:384]
                kvp = v3(bank(6, 2), "p (t h d) -> p t h d", t=TT, h=H)
                a.activation(q_tok[:, :, :, 0:HD], v3(qp, "p t (h d) -> p t h d", h=H)[:, :, :, 0:HD], ACT.Copy)
                a.activation(k_tok[:, :, :, 0:HD], kvp[:, :, :, 0:HD], ACT.Copy)
                a.activation(vm[:, :, :, 0:HD], kvp[:, :, :, HD:2 * HD], ACT.Copy).then_inc(sem["mla_nope"], 1)
                split_mid(7)
                evac(5)
                split_mid(8)
                evac(6)
                act.wait_ge(*E.at("s5_y", 1))
                act.wait_ge(*E.at("s5_x", 1))
                a.activation(s_tmp[0], bank(4), ACT.Copy).then_inc(sem["s5_yc"], 1)
                act.wait_ge(*E.at("mla_t2", 1))
                a.activation(qk_a[0:MLA_D, 0:H * S], bank(2, 2)[0:MLA_D], ACT.Copy).then_inc(sem["mla_qt"], 1)
                act.wait_ge(*E.at("s5_ga", 1))
                a.activation(s_tmp[2], s_tmp[1], ACT.Tanh, scale=GELU_S).then_inc(sem["s5_th"], 1)
                def attention(g):
                    act.wait_ge(*E.at("att_max", POS[g] + 1))
                    for hh in range(H):
                        a.activation(probs[:, hh * S:(hh + 1) * S], s1[:, hh], ACT.Exp, scale=SCALE[g],
                                     bias=nb[:, hh:hh + 1])
                    for hh in range(H):
                        i = a.activation(probs[:, 1024 + hh * P:1024 + (hh + 1) * P], s0[:, hh], ACT.Exp,
                                         scale=SCALE[g], bias=nb[:, 4 + hh:5 + hh])
                    i.then_inc(sem["att_exp"], 1)

                def attention_t(g):
                    act.wait_ge(*E.at("att_t", POS[g] + 1))
                    a.activation(probs_t[:, 0:512], bank(5), ACT.Copy).then_inc(sem["att_tc_act"], 1)

                def evac_kv(m):
                    s, n, _ = mid(m)
                    q = KV_UNITS.index(m)
                    act.wait_ge(*E.at(unit_done[s], n + 1))
                    if q == 4:
                        act.wait_ge(*E.at("x_split", FILL[FI_MEM] + KT))
                    if q < 4:
                        i = a.activation(zone[:, q * 512:(q + 1) * 512], bank(KV_BANK[q]), ACT.Copy)
                    else:
                        i = a.activation(xv[:, :, (q - 4) * UC:(q - 3) * UC],
                                         v3(bank(KV_BANK[q]), "p (t n) -> p t n", t=TT), ACT.Copy)
                    i.then_inc(sem["xkv_done"], 1)

                act.dma_start(zone[:, 2048:4096], mem_scratch).then_inc(sem["mem_in"], 16)
                split_mid(9)
                evac(7)
                act.wait_ge(*E.at("s5_g", 1))
                g_from = v3(s_tmp[3], "p (i a q) -> p a i q", i=2, a=4)
                y_to = v3(work[:, 0:512], "p (i q r) -> p i q r", i=2, r=CH)
                for r in range(2):
                    for q in range(4):
                        i = a.activation(y_to[32 * q:32 * q + 32, :, :, r], g_from[32 * r:32 * r + 32, q],
                                         ACT.Copy, scale=0.5)
                i.then_inc(sem["s5_sc_act"], 1)
                attention(0)
                act.wait_ge(*E.at("fox_x", 1))
                a.activation(f_b2, f_a, ACT.Exp).then_inc(sem["fox_e"], 1)
                act.wait_ge(*E.at("fox_e", 1))
                a.activation(f_a, f_b2, ACT.Ln, bias=1.0).then_inc(sem["fox_ln"], 1)
                evac(8)
                act.wait_ge(*E.at("mem_in", 16))
                for k in range(KT):
                    a.activation(xh3[:, k], zone[:, 2048 + k * S:2048 + (k + 1) * S], ACT.Copy,
                                     scale=pcol[:, C_MEM + k:C_MEM + k + 1]).then_inc(sem["x_hi_done"], 1)
                act.wait_ge(*E.at("nsa_t", 1))
                a.activation(kc2[0:HD, :], bank(6)[0:HD], ACT.Copy).then_inc(sem["nsa_kc"], 1)
                a.activation(nsa_q[0:HD, :], bank(2, 2)[0:HD], ACT.Copy).then_inc(sem["nsa_tc_act"], 1)
                act.wait_ge(*E.at("s5_z", 1))
                for i_ in range(2):
                    i = a.activation(s_tmp[1][:, i_ * S:(i_ + 1) * S], bank(5)[:, i_ * S:(i_ + 1) * S], ACT.Tanh,
                                     scale=0.5, bias=half_b[:, i_:i_ + 1])
                i.then_inc(sem["s5_zt"], 1)
                act.wait_ge(*E.at("gate_x", 1))
                a.activation(gates, gates, ACT.Tanh, scale=0.5).then_inc(sem["gate_th"], 1)
                evac_kv(9)
                attention_t(0)
                act.wait_ge(*E.at("fox_cum", 1))
                a.activation(ncum, bank(5)[:, 0:S], ACT.Copy,
                                 scale=-1.0 / SCALE[3]).then_inc(sem["fox_nc"], 1)
                act.wait_ge(*E.at("fox_tq", 1))
                a.activation(qk_a[0:HD, 0:H * S], bank(6, 2)[0:HD], ACT.Copy).then_inc(sem["fox_qt"], 1)
                split_mid(14)
                split_mid(15)
                attention(3)
                act.wait_ge(*E.at("phi_x", 1))
                a.activation(v3(hx2, "p (a n) -> p a n", n=NC_CMP), v3(hx2, "p (a n) -> p a n", n=NC_CMP),
                                 ACT.Tanh, scale=GELU_S).then_inc(sem["phi_th"], 1)
                split_mid(16)
                evac_kv(14)
                attention_t(3)
                split_mid(17)
                evac_kv(15)
                act.wait_ge(*E.at("phi_out", 1))
                a.activation(kct[0:HD, 0:NC_CMP], bank(5)[0:HD, 0:NC_CMP], ACT.Copy, scale=0.5)
                a.activation(vct[0:NC_CMP], bank(5)[0:NC_CMP, 64:128], ACT.Copy, scale=0.5).then_inc(sem["phi_c"], 1)
                split_mid(18)
                evac_kv(16)
                split_mid(19)
                attention(1)
                act.wait_ge(*E.at("cmp_x", 1))
                a.activation(cp, cp, ACT.Exp).then_inc(sem["cmp_e"], 1)
                evac_kv(17)
                attention_t(1)
                split_mid(20)
                evac_kv(18)
                act.wait_ge(*E.at("cmp_t", 1))
                a.activation(probs_t[0:NC_CMP, 0:1024], bank(6, 2)[0:NC_CMP], ACT.Copy).then_inc(sem["cmp_tc"], 1)
                split_mid(21)
                evac_kv(19)
                split_mid(22)
                attention(2)
                evac_kv(20)
                attention_t(2)
                split_mid(23)

                act.wait_ge(*E.at("att_out", 4))
                for t in range(TT):
                    for q in range(3):
                        i = a.activation(probs[:, (t * 3 + q) * 256:(t * 3 + q + 1) * 256],
                                         mix_out[:, (t * 3 + q) * 256:(t * 3 + q + 1) * 256],
                                         ACT.Square, accum_out=ss[N_GRP][:, t * 3 + q:t * 3 + q + 1])
                i.then_inc(sem["grp_sq"], 1)
                s, n, _ = mid(20)
                act.wait_ge(*E.at(unit_done[s], n + 1))
                act.wait_ge(*E.at("s5_out", 1))
                for k in (6, 7):
                    a.activation(xh3[:, k], s_out[:, k - 6], ACT.Copy).then_inc(sem["x_hi_done"], 1)
                for k in range(6):
                    if k % 2 == 0:
                        act.wait_ge(*E.at("grp_t", k // 2 + 1))
                    a.activation(xh3[:, k], rows_of_t[:, k], ACT.Copy, scale=pcol[:, C_GRP + k:C_GRP + k + 1]).then_inc(sem["x_hi_done"], 1)
                for m in range(21, 25):
                    if m >= 22:
                        split_mid(m + 2)
                y_squares(1)
                h_squares(2)
                fill_hi(2)
                load_gain(2)

                def xa_exp(q):
                    act.wait_ge(*E.at("xmax", q + 1))
                    for t in range(TT):
                        i = a.activation(probs[:, (q % 2) * 512 + t * S:(q % 2) * 512 + (t + 1) * S],
                                         bank(6 + q % 2)[:, t * S:(t + 1) * S], ACT.Exp, scale=256 ** -0.5,
                                         bias=nb[:, 2 * q + t:2 * q + t + 1],
                                         accum_out=rc[:, 2 * q + t:2 * q + t + 1])
                    i.then_inc(sem["xexp"], 1)

                def xa_out(q):
                    act.wait_ge(*E.at("xo", q + 1))
                    a.activation(work[:, q * 512:(q + 1) * 512], bank(q % 2), ACT.Copy).then_inc(sem["xoc"], 1)

                for q in range(4):
                    m = M_Q + q
                    split_mid(m + 2)
                    s, n, _ = mid(m)
                    act.wait_ge(*E.at(unit_done[s], n + 1))
                    a.activation(proj[:, q * 512:(q + 1) * 512], bank(4 + q % 2), ACT.Copy).then_inc(sem["xq_done"], 1)
                    xa_exp(q)
                    if q >= 2:
                        xa_out(q - 2)
                xa_out(2)
                xa_out(3)
                for q in range(4):
                    act.wait_ge(*E.at("xoc", q + 1))
                    if q == 0:
                        s, n, _ = mid(28)
                        act.wait_ge(*E.at(unit_done[s], n + 1))
                    a.activation(x_hi[:, q * 512:(q + 1) * 512], work[:, q * 512:(q + 1) * 512], ACT.Copy).then_inc(sem["x_hi_done"], 1)
                split_mid(31)
                split_mid(32)
                split(*ffn_base(1)[0])
                split(*ffn_base(1)[1])
                y_squares(2)
                h_squares(3)

                fill_hi(3)
                load_gain(3)
                act.wait_ge(*E.at("x_split", FILL[FI_F2] + KT))
                act.dma_start(pcol[:, :], cols[l + 1]).then_inc(sem["pcol_in"], 16)
                act.dma_start(pmat[:, :], mats[l + 1]).then_inc(sem["pmat_in"], 16)
                ffn_piece(1, 0, False)
                with act.Fori(1, FU - 1) as i:
                    ffn_piece(1, i, False)
                    act.wait_ge(s_con, 16)
                ffn_piece(1, FU - 1, True)
                ffn_tail(1)
                y_squares(3)
                act.wait_ge(*E.at("pcol_in", 16))
                act.wait_ge(*E.at("pmat_in", 16))
                act.wait_ge(*E.at("h_done", 8))
                act.wait_ge(s_con, 16)
            act.dma_start(out.rearrange("(t p) d -> p t d", p=P), h3).then_inc(out_stored, 16)
            act.wait_ge(out_stored, 16)

        @block.vector
        def _(dve):
            v = nc.vector
            dve.wait_ge(b_ss, 1)
            v.tensor_scalar(ss[0], ss[0], 1.0 / D, EPS, ALU.mult, ALU.add).then_inc(b_var, 1)
            dve.wait_ge(b_rstd, 1)
            for t in range(TT):
                v.tensor_scalar(w3[:, t], w3[:, t], rstd[0][:, t:t + 1], None, ALU.mult).then_inc(b_xn, 1)
            with dve.Fori(0, DEPTH) as l:
                E = Engine(dve, "dve", l)

                def tt(o, x_, y_, op):
                    return v.tensor_tensor(o, x_, y_, op)

                def stt(o, x_, s_, y_, op0, op1):
                    return v.scalar_tensor_tensor(out=o, in0=x_, scalar=s_, in1=y_, op0=op0, op1=op1)

                def split(s, ns, w=UC):
                    dve.wait_ge(*E.at(hi_done[s], ns + 1))
                    o, i, j = (v3(x_, "p (k n) -> p k n", n=UC)[:, :, 0:w] for x_ in (w_lo[s][:, :], raw[s][:, :], w_f[s]))
                    tt(o, i, j, ALU.subtract).then_inc(sem[split_done[s]], 1)

                def split_mid(m):
                    s, n, ns = mid(m)
                    split(s, ns, IN_W[m] if m < N_IN else UC)

                def variance(n, parts):
                    for (a_, b_), w in parts:
                        i = v.tensor_scalar(ss[n][:, a_:b_], ss[n][:, a_:b_], 1.0 / w, EPS, ALU.mult, ALU.add)
                    i.then_inc(sem["var_done"], 1)

                def normed_rows(p):
                    n = PRE[p][0]
                    for t in range(TT):
                        dve.wait_ge(*E.at("rstd_done", RSTD[n] + t + 1))
                        v.tensor_scalar(w3[:, t], h3[:, t], rstd[n][:, t:t + 1], None, ALU.mult).then_inc(sem["xn_ready"], 1)

                def fill_lo(p):
                    n, fi, gc = PRE[p]
                    for k in range(KT):
                        if k % 2 == 0:
                            dve.wait_ge(*E.at("x_hi_done", FILL[fi] + k + 2))
                        stt(xl3[:, k], rows_of_t[:, k], pcol[:, gc + k:gc + k + 1], x_f[:, k],
                                ALU.mult, ALU.subtract).then_inc(sem["x_split"], 1)

                def post_norm(q, weight):
                    n = POST[q]
                    dve.wait_ge(*E.at("gain_in", 16 * (q + 1)))
                    for t in range(TT):
                        dve.wait_ge(*E.at("y_sq", 2 * q + t + 1))
                        E.step(stt(w3[:, t], y_ps[:, t], weight, gain[:, :], ALU.mult, ALU.mult))
                        dve.wait_ge(*E.at("rstd_done", RSTD[n] + t + 1))
                        stt(h3[:, t], w3[:, t], rstd[n][:, t:t + 1], h3[:, t], ALU.mult, ALU.add).then_inc(sem["h_done"], 1)
                    dve.wait_ge(*E.at("h_done", 2 * q + 2))

                def ffn_piece(f, i, last):
                    (g_, g, gs), (u_, u, us), (d_, d, ds), (z_, _, zs) = ffn_base(f)
                    if not isinstance(i, int) or i > 0:
                        split(d_, ds - 1 + i)
                        dve.wait_ge(*E.at("hid_hi_done", f * FU + i))
                        tt(hid_lo[:, :], f_hid, hid_f, ALU.subtract).then_inc(sem["hid_split"], 1)
                    if not last:
                        split(g_, gs + 1 + i)
                    dve.wait_ge(*E.at("tanh_done", f * FU + 1 + i))
                    stt(f_t, f_th, 1.0, bank(4), ALU.add, ALU.mult).then_inc(sem["gated"], 1)
                    if last:
                        split(z_, zs)
                    dve.wait_ge(*E.at("gated", f * FU + 1 + i))
                    dve.wait_ge(*E.at(unit_done[u_], u + 1 + i))
                    if not isinstance(i, int) or i > 0:
                        dve.wait_ge(*E.at("hid_split", f * FU + i))
                    stt(f_hid, f_t, 0.5, bank(5), ALU.mult, ALU.mult).then_inc(sem["hid_done"], 1)
                    if not last:
                        split(u_, us + 1 + i)

                def ffn_tail(f):
                    dve.wait_ge(*E.at("hid_hi_done", f * FU + FU))
                    tt(hid_lo[:, :], f_hid, hid_f, ALU.subtract).then_inc(sem["hid_split"], 1)

                normed_rows(0)
                split(0, 0)
                fill_lo(0)
                split(1, 0)
                ffn_piece(0, 0, False)
                with dve.Fori(1, FU - 1) as i:
                    ffn_piece(0, i, False)
                    dve.wait_ge(s_con, 16)
                ffn_piece(0, FU - 1, True)
                ffn_tail(0)
                split_mid(0)
                split_mid(1)
                post_norm(0, 0.5)
                normed_rows(1)
                fill_lo(1)

                split_mid(2)
                dve.wait_ge(*E.at("proj_done", 1))
                u_ps = v3(bank(0), "p (i q r) -> p i q r", i=2, r=CH)
                u_to = v3(s_u.rearrange("p g q -> p (g q)"), "p (i a q) -> p a i q", i=2, a=4)
                for j in (2, 3):
                    for q in range(4):
                        i = v.tensor_copy(u_to[32 * j:32 * j + 32, q], u_ps[32 * q:32 * q + 32, :, :, CH - 1 - j])
                i.then_inc(sem["s5_u_dve"], 1)
                split_mid(3)
                split_mid(4)
                dve.wait_ge(*E.at("mla_sq", 1))
                variance(N_MLA, [((0, 2), MLA_Q), ((2, 4), MLA_KV)])
                dve.wait_ge(*E.at("rstd_done", RSTD[N_MLA] + 1))
                for q, (lo, w) in enumerate(((I_CQ, MLA_Q), (I_CKV, MLA_KV))):
                    i = tt(pr3[:, :, lo:lo + w], pr3[:, :, lo:lo + w],
                           bc(rstd[N_MLA][:, 2 * q:2 * q + 2], 2, w), ALU.mult)
                i.then_inc(sem["mla_xn"], 1)
                dve.wait_ge(*E.at("s5_t", 1))
                dve.wait_ge(*E.at("s5_k", 1))
                v.tensor_copy(zone[:, 1024:2048], bank(6, 2)).then_inc(sem["s5_lb_dve"], 1)
                tt(k_ps[:, :, 0:C2], k_ps[:, :, 0:C2], v3(pmat[:, W_D:W_D + PAIRS * C2], "p (g c) -> p g c",
                                                                g=PAIRS), ALU.add).then_inc(sem["s5_kd"], 1)
                split_mid(5)
                dve.wait_ge(*E.at("s5_kd", 1))
                for j in (0, 1):
                    i = v.tensor_copy(s_t0[32 * j:32 * j + 32, :, CH - 1 - j:CH, :],
                                      v3(bank(2, 2), "p (g r c) -> p g r c", g=PAIRS, r=CH)
                                      [32 * j:32 * j + 32, :, 0:j + 1, :])
                i.then_inc(sem["s5_t0_dve"], 1)
                sn, cs = zone[:, 3584:4096], zone[:, 3072:3584]
                dve.wait_ge(*E.at("s5_v", 1))
                tt(s_tmp[0], bank(4), cs, ALU.mult)
                tt(s_tmp[1], bank(5), sn, ALU.mult)
                tt(s_tmp[2], bank(5), cs, ALU.mult)
                E.step(tt(s_tmp[3], bank(4), sn, ALU.mult))
                tt(s_tmp[0], s_tmp[0], s_tmp[1], ALU.add)
                E.step(tt(s_tmp[2], s_tmp[2], s_tmp[3], ALU.subtract))
                v.tensor_tensor_scan(s_tmp[1], kc2[:, :], s_tmp[0], 0.0, ALU.mult, ALU.add)
                E.step(v.tensor_tensor_scan(s_tmp[3], kc2[:, :], s_tmp[2], 0.0, ALU.mult, ALU.add))
                split_mid(6)
                tt(s_tmp[0], s_tmp[1], cs, ALU.mult)
                E.step(tt(s_tmp[2], s_tmp[3], sn, ALU.mult))
                tgq = [v3(x_, "p (g q) -> p g q", g=PAIRS) for x_ in s_tmp]
                E.step(tt(s_x[0][:, :, 1:NCH + 1], tgq[0], tgq[2], ALU.subtract))
                tt(s_tmp[0], s_tmp[1], sn, ALU.mult)
                E.step(tt(s_tmp[2], s_tmp[3], cs, ALU.mult))
                tt(s_x[1][:, :, 1:NCH + 1], tgq[0], tgq[2], ALU.add).then_inc(sem["s5_x"], 1)
                dve.wait_ge(*E.at("mla_nope", 1))
                mcc, mss = (v3(con[:, c_:c_ + TT * MLA_R], "p (t d) -> p t d", t=TT) for c_ in (K_MCC, K_MSS))
                r1, r2 = (v3(rope_t[:, 512 + i_ * 256:768 + i_ * 256], "p (t h d) -> p t h d", t=TT, h=H)
                          for i_ in range(2))
                R2 = MLA_R // 2
                q_pe = v3(v3(bank(2, 2), "p (t n) -> p t n", t=TT)[:, :, 0:384], "p t (h d) -> p t h d", h=H)[
                    :, :, :, HD:]
                tt(r1, q_pe, bc(mcc, 2, H), ALU.mult)
                E.step(tt(r2, q_pe, bc(mss, 2, H), ALU.mult))
                tt(q_tok[:, :, :, HD:HD + R2], r1[:, :, :, 0:R2], r2[:, :, :, R2:], ALU.subtract)
                E.step(tt(q_tok[:, :, :, HD + R2:], r2[:, :, :, 0:R2], r1[:, :, :, R2:], ALU.add))
                k_pe = pr3[:, :, I_KPE:I_NQ]
                tt(r1[:, :, 0], k_pe, mcc, ALU.mult)
                E.step(tt(r2[:, :, 0], k_pe, mss, ALU.mult))
                tt(k_tok[:, :, :, HD:HD + R2], bc(r1[:, :, 0, 0:R2], 2, H), bc(r2[:, :, 0, R2:], 2, H), ALU.subtract)
                tt(k_tok[:, :, :, HD + R2:], bc(r2[:, :, 0, 0:R2], 2, H), bc(r1[:, :, 0, R2:], 2, H), ALU.add).then_inc(sem["mla_tok"], 1)
                split_mid(7)
                dve.wait_ge(*E.at("proj_done", 6))
                dve.wait_ge(*E.at("s5_y", 1))
                dve.wait_ge(*E.at("mla_tok", 1))
                ncc, nss = (v3(con[:, c_:c_ + TT * HD], "p (t d) -> p t d", t=TT) for c_ in (K_NCC, K_NSS))
                R2 = HD // 2
                for x_, n_ in ((v3(pr3[:, :, I_NQ:I_KC], "p t (h d) -> p t h d", d=HD), H),
                               (v3(pr3[:, :, I_KC:I_KC + 384], "p t (h d) -> p t h d", d=2 * HD)[:, :, :, 0:HD], 3)):
                    r1, r2 = (v3(rope_t[:, i_ * 512:i_ * 512 + TT * n_ * HD], "p (t h d) -> p t h d", t=TT, h=n_)
                              for i_ in range(2))
                    tt(r1, x_, bc(ncc, 2, n_), ALU.mult)
                    E.step(tt(r2, x_, bc(nss, 2, n_), ALU.mult))
                    tt(x_[:, :, :, 0:R2], r1[:, :, :, 0:R2], r2[:, :, :, R2:], ALU.subtract)
                    i = tt(x_[:, :, :, R2:], r2[:, :, :, 0:R2], r1[:, :, :, R2:], ALU.add)
                    if n_ == H:
                        E.step(i)
                    else:
                        i.then_inc(sem["nsa_rope"], 1)
                gb = v3(pcol[:, C_GB:C_GB + 3 * H], "p (b h) -> p b h", b=3)
                tt(gates, v3(pr3[:, :, I_G:I_FQ], "p t (b h) -> p t b h", b=3), bc(gb, 1, TT), ALU.add).then_inc(sem["gate_x"], 1)
                v.tensor_scalar(half_b, pcol[:, C_GLUB:C_GLUB + 2], 0.5, None, ALU.mult)
                E.step(tt(flog, flog, bc(pcol[:, C_FB:C_FB + H], 1, TT), ALU.add))
                stt(f_a, flog, -1.0, flog, ALU.mult, ALU.min).then_inc(sem["fox_x"], 1)
                E.step(v.tensor_scalar(flog, flog, 0.0, None, ALU.min))
                split_mid(8)
                dve.wait_ge(*E.at("mla_t2", 1))
                v.tensor_copy(qk_a[0:MLA_D, H * S:], bank(6, 2)[0:MLA_D]).then_inc(sem["mla_kt"], 1)
                dve.wait_ge(*E.at("s5_yc", 1))
                E.step(tt(s_tmp[1], s_tmp[0], s_tmp[0], ALU.mult))
                E.step(v.tensor_scalar(s_tmp[1], s_tmp[1], GELU_A, 1.0, ALU.mult, ALU.add))
                tt(s_tmp[1], s_tmp[1], s_tmp[0], ALU.mult).then_inc(sem["s5_ga"], 1)
                dve.wait_ge(*E.at("s5_th", 1))
                stt(s_tmp[3], s_tmp[2], 1.0, s_tmp[0], ALU.add, ALU.mult).then_inc(sem["s5_g"], 1)
                dve.wait_ge(*E.at("s5_g", 1))
                g_from = v3(s_tmp[3], "p (i a q) -> p a i q", i=2, a=4)
                y_to = v3(work[:, 0:512], "p (i q r) -> p i q r", i=2, r=CH)
                for r in (2, 3):
                    for q in range(4):
                        i = v.tensor_scalar(y_to[32 * q:32 * q + 32, :, :, r], g_from[32 * r:32 * r + 32, q],
                                            0.5, None, ALU.mult)
                i.then_inc(sem["s5_sc_dve"], 1)
                def attention_max(g):
                    dve.wait_ge(*E.at("att_s", POS[g] + 1))
                    tt(s1[:, :, P:S], s1[:, :, P:S], bc(mask, 1, H), ALU.add)
                    E.step(tt(s0, s0, bc(mask, 1, H), ALU.add))
                    v.reduce_max(mx[:, 0:4], s1, AX.X)
                    E.step(v.reduce_max(mx[:, 4:8], s0, AX.X))
                    if g < 3:
                        i = v.tensor_scalar(nb, mx, -SCALE[g], None, ALU.mult)
                    else:
                        E.step(stt(mx, mx, SCALE[g], cumt, ALU.mult, ALU.add))
                        i = tt(nb, cumt, mx, ALU.subtract)
                    i.then_inc(sem["att_max"], 1)

                def attention_copy(g):
                    dve.wait_ge(*E.at("att_t", POS[g] + 1))
                    v.tensor_copy(probs_t[:, 512:1536], bank(6, 2)).then_inc(sem["att_tc_dve"], 1)

                def attention_out(g):
                    dve.wait_ge(*E.at("att_pv", POS[g] + 1))
                    r_ = v3(rc, "p (t h) -> p t h", t=TT)
                    for t in range(TT):
                        i = v.tensor_scalar(r_[:, t].unsqueeze(2), o_ps[t][:, :, HD:HD + 1], 1e-30, None, ALU.max)
                    E.step(i)
                    E.step(v.reciprocal(rc, rc))
                    if g in (1, 2):
                        E.step(tt(r_, r_, gates[:, :, g], ALU.mult))
                    o_t = v3(rope_t[:, 256:768], "p (t h d) -> p t h d", t=TT, h=H)
                    to = mo[:, :, (0, 1, 1, 2)[g]]
                    for t in range(TT):
                        i = tt(o_t[:, t] if g == 2 else to[:, t], o_ps[t][:, :, 0:HD], bc(r_[:, t], 2, HD), ALU.mult)
                    if g == 2:
                        E.step(i)
                        i = tt(to, to, o_t, ALU.add)
                    i.then_inc(sem["att_out"], 1)
                    dve.wait_ge(*E.at("att_out", POS[g] + 1))

                attention_max(0)
                E.step(v.memset(rope_t[:, 768:1024], 0.0))
                dve.wait_ge(*E.at("fox_ln", 1))
                tt(lf[:, :, 0:P:32], flog, f_a, ALU.subtract).then_inc(sem["fox_lf"], 1)
                split_mid(9)
                for k in range(KT):
                    dve.wait_ge(*E.at("x_hi_done", FILL[FI_MEM] + k + 1))
                    stt(xl3[:, k], zone[:, 2048 + k * S:2048 + (k + 1) * S], pcol[:, C_MEM + k:C_MEM + k + 1],
                            x_f[:, k], ALU.mult, ALU.subtract).then_inc(sem["x_split"], 1)
                dve.wait_ge(*E.at("nsa_t", 1))
                v.tensor_copy(nsa_k[0:HD, :], bank(7)[0:HD])
                dve.wait_ge(*E.at("nsa_kc", 1))
                i = v.tensor_copy(kc[HD:P, :, 0:S - 1], v3(bank(6), "p (j s) -> p j s", j=2)[0:HD, :, 1:S])
                i.then_inc(sem["nsa_tc_dve"], 1)
                dve.wait_ge(*E.at("nsa_tc_dve", 1))
                for j in range(2):
                    t16 = kc[:, j].rearrange("p (n r) -> p r n", r=CMP_STRIDE)
                    for half in range(2):
                        ks = slice(half * 8, half * 8 + 8)
                        pos = pcol[:, C_POS + j * CMP_KT + half * 8:C_POS + j * CMP_KT + half * 8 + 8]
                        i = tt(bl[:, j, ks], t16[:, 0:CMP_STRIDE:2, half:half + NC_CMP], bc(pos, 2, NC_CMP), ALU.add)
                i.then_inc(sem["blocks_done"], 1)
                attention_copy(0)
                dve.wait_ge(*E.at("s5_zt", 1))
                E.step(stt(s_tmp[2], s_tmp[1], 1.0, s_tmp[0], ALU.add, ALU.mult))
                E.step(v.tensor_scalar(s_tmp[3], s_tmp[2], 0.5, None, ALU.mult))
                tt(s_tmp[2], s_tmp[3], s_tmp[3], ALU.mult).then_inc(sem["s5_sq"], 1)
                dve.wait_ge(*E.at("gate_th", 1))
                v.tensor_scalar(gates, gates, 0.5, 0.5, ALU.mult, ALU.add).then_inc(sem["gates_done"], 1)
                dve.wait_ge(*E.at("gates_done", 1))
                attention_out(0)
                dve.wait_ge(*E.at("fox_nc", 1))
                v.tensor_copy(cumt, bank(5)[:, 256:264]).then_inc(sem["fox_ct"], 1)
                dve.wait_ge(*E.at("s5_ss", 1))
                v.tensor_scalar(s5_r, bank(1)[:, S:S + TT], 1.0 / 256, EPS, ALU.mult, ALU.add).then_inc(sem["s5_var"], 1)
                dve.wait_ge(*E.at("fox_tk", 1))
                v.tensor_copy(qk_a[0:HD, H * S:], bank(2, 2)[0:HD]).then_inc(sem["fox_kt"], 1)
                dve.wait_ge(*E.at("s5_rstd_all", 1))
                for k in range(2):
                    i = stt(s_out[:, k], s_out[:, k], pcol[:, C_GRP + 6 + k:C_GRP + 7 + k], bank(1)[:, 0:S],
                            ALU.mult, ALU.mult)
                i.then_inc(sem["s5_out"], 1)
                split_mid(14)
                dve.wait_ge(*E.at("fox_ct", 1))
                attention_max(3)
                split_mid(15)
                s, n, _ = mid(M_PHI + 3)
                dve.wait_ge(*E.at(unit_done[s], n + 1))
                hx3, hy3 = (v3(x_, "p (a n) -> p a n", n=NC_CMP) for x_ in (hx, hx2))
                E.step(tt(hx3, v3(bank(0)[:, 0:64], "p (a n) -> p a n", n=16)[:, :, 0:NC_CMP],
                          bc(pcol[:, C_PHIB:C_PHIB + 4], 2, NC_CMP), ALU.add))
                E.step(tt(hx2, hx, hx, ALU.mult))
                E.step(v.tensor_scalar(hx2, hx2, GELU_A, 1.0, ALU.mult, ALU.add))
                tt(hx2, hx2, hx, ALU.mult).then_inc(sem["phi_x"], 1)
                dve.wait_ge(*E.at("phi_th", 1))
                stt(hx, hx2, 1.0, hx, ALU.add, ALU.mult).then_inc(sem["phi_hid"], 1)
                split_mid(16)
                attention_copy(3)
                split_mid(17)
                attention_out(3)
                split_mid(18)
                attention_max(1)
                dve.wait_ge(*E.at("cmp_s", 1))
                c01, cng = (v3(con[:, c_:c_ + TT * NC_CMP], "p (t n) -> p t n", t=TT) for c_ in (K_C01, K_CNEG))
                for t in range(TT):
                    i = stt(cp[:, t * H:(t + 1) * H], c_ps[:, t * H:(t + 1) * H, 0:NC_CMP], HD ** -0.5,
                            bc(cng[:, t], 1, H), ALU.mult, ALU.add)
                E.step(i)
                E.step(v.reduce_max(cq8, cp, AX.X))
                tt(cp, cp, bc(cq8, 2, NC_CMP), ALU.subtract).then_inc(sem["cmp_x"], 1)
                split_mid(19)
                attention_copy(1)
                dve.wait_ge(*E.at("cmp_e", 1))
                cpt = v3(rope_t[:, 128:248], "p (t h n) -> p t h n", t=TT, h=H)
                E.step(tt(cpt, cpt, bc(c01, 2, H), ALU.mult))
                E.step(v.reduce_sum(cs8, cp, AX.X))
                E.step(v.tensor_scalar(cs8, cs8, 1e-30, None, ALU.max))
                E.step(v.reciprocal(cs8, cs8))
                c8 = v3(cs8, "p (t h) -> p t h", t=TT)
                E.step(tt(c8, c8, gates[:, :, 0], ALU.mult))
                tt(cp, cp, bc(cs8, 2, NC_CMP), ALU.mult).then_inc(sem["cmp_p"], 1)
                split_mid(20)
                attention_out(1)
                split_mid(21)
                attention_max(2)
                dve.wait_ge(*E.at("cmp_o", 1))
                tt(mo[:, :, 1], mo[:, :, 1], v3(bank(5), "p (t h d) -> p t h d", t=TT, h=H), ALU.add).then_inc(sem["cmp_done"], 1)
                dve.wait_ge(*E.at("cmp_done", 1))
                split_mid(22)
                attention_copy(2)
                split_mid(23)
                attention_out(2)

                dve.wait_ge(*E.at("grp_sq", 1))
                variance(N_GRP, [((0, 6), 256)])
                dve.wait_ge(*E.at("rstd_done", RSTD[N_GRP] + 1))
                m6 = v3(mix_out[:, :], "p (a n) -> p a n", a=6)
                tt(m6, m6, bc(rstd[N_GRP], 2, 256), ALU.mult).then_inc(sem["grp_xn"], 1)
                for n_, k in enumerate(MO_ORDER):
                    if n_ % 2 == 0:
                        dve.wait_ge(*E.at("x_hi_done", FILL[FI_MO] + n_ + 2))
                    if k >= 6:
                        i = tt(xl3[:, k], s_out[:, k - 6], x_f[:, k], ALU.subtract)
                    else:
                        i = stt(xl3[:, k], rows_of_t[:, k], pcol[:, C_GRP + k:C_GRP + k + 1], x_f[:, k],
                                ALU.mult, ALU.subtract)
                    i.then_inc(sem["x_split"], 1)
                for m in range(22, 25):
                    split_mid(m + 2)
                post_norm(1, 1.0)
                normed_rows(2)
                fill_lo(2)

                def xa_max(q):
                    dve.wait_ge(*E.at("xs", q + 1))
                    E.step(v.reduce_max(mx[:, 2 * q:2 * q + 2], v3(bank(6 + q % 2), "p (t s) -> p t s", t=TT), AX.X))
                    v.tensor_scalar(nb[:, 2 * q:2 * q + 2], mx[:, 2 * q:2 * q + 2], -256 ** -0.5, None, ALU.mult).then_inc(sem["xmax"], 1)

                def xa_probs(q):
                    dve.wait_ge(*E.at("xexp", q + 1))
                    E.step(v.reciprocal(rc[:, 2 * q:2 * q + 2], rc[:, 2 * q:2 * q + 2]))
                    p_ = v3(probs[:, (q % 2) * 512:(q % 2 + 1) * 512], "p (t s) -> p t s", t=TT)
                    tt(p_, p_, bc(rc[:, 2 * q:2 * q + 2], 2, S), ALU.mult).then_inc(sem["xp"], 1)

                def xa_copy(q):
                    dve.wait_ge(*E.at("xt", q + 1))
                    v.tensor_copy(probs_t[:, (q % 2) * 512:(q % 2 + 1) * 512], bank(2 + q % 2)).then_inc(sem["xtc"], 1)

                for q in range(4):
                    split_mid(M_Q + q + 2)
                    xa_max(q)
                    xa_probs(q)
                    if q >= 1:
                        xa_copy(q - 1)
                xa_copy(3)
                for q in range(4):
                    dve.wait_ge(*E.at("x_hi_done", FILL[FI_XO] + q + 1))
                    tt(x_lo[:, q * 512:(q + 1) * 512], work[:, q * 512:(q + 1) * 512],
                           x_hi[:, q * 512:(q + 1) * 512].bitcast(F32), ALU.subtract).then_inc(sem["x_split"], 1)
                split_mid(31)
                split_mid(32)
                for s, _, ns in ffn_base(1)[:2]:
                    split(s, ns)
                post_norm(2, 1.0)

                normed_rows(3)
                fill_lo(3)
                ffn_piece(1, 0, False)
                with dve.Fori(1, FU - 1) as i:
                    ffn_piece(1, i, False)
                    dve.wait_ge(s_con, 16)
                ffn_piece(1, FU - 1, True)
                ffn_tail(1)
                post_norm(3, 0.5)
                dve.wait_ge(s_con, 16)
                E.end()

        @block.tensor
        def _(pe):
            t_ = nc.tensor
            pe.wait_ge(s_con, 16)
            pe.wait_ge(b_xn, 2)
            for k in range(KT):
                for t in range(TT):
                    i = t_.transpose(rows_of_t[:, k, t * P:(t + 1) * P], w3[:, t, k * P:(k + 1) * P], ident)
            i.then_inc(b_t, 1)
            pe.wait_ge(b_tc, 1)
            pe.wait_ge(b_one, 1)
            with pe.Fori(0, DEPTH) as l:
                E = Engine(pe, "pe", l)

                def mm(o, a_, b_, first, last):
                    return t_.matmul(o, a_, b_, start=first, stop=last)

                def three(terms, o, first=True, last=True):
                    n = len(terms)
                    for q, ((ah, al), (bh, bl_)) in enumerate(terms):
                        mm(o, ah, bh, first and q == 0, False)
                        mm(o, ah, bl_, False, False)
                        i = mm(o, al, bh, False, last and q == n - 1)
                    return i

                def unit_feature(s, n, ns, o, fill=None):
                    pe.wait_ge(*E.at(split_done[s], ns + 1))
                    for j in range(2):
                        for k in range(KT):
                            if fill is not None and j == 0 and k % 2 == 0:
                                pe.wait_ge(*E.at("x_split", FILL[fill] + k + 2))
                            i = three([((w_hi[s][:, k * UC + j * P:k * UC + (j + 1) * P],
                                         w_lo[s][:, k * UC + j * P:k * UC + (j + 1) * P]), (xh3[:, k], xl3[:, k]))],
                                      o[:, j * S:(j + 1) * S], k == 0, k == KT - 1)
                    i.then_inc(sem[unit_done[s]], 1)

                def unit_tokens(s, n, ns, o, w, fill=None):
                    pe.wait_ge(*E.at(split_done[s], ns + 1))
                    if fill is not None:
                        pe.wait_ge(*E.at("x_split", FILL[fill] + KT))
                    for t in range(TT):
                        i = three([((xh3[:, k, t * P:(t + 1) * P], xl3[:, k, t * P:(t + 1) * P]),
                                    (w_hi[s][:, k * UC:k * UC + w], w_lo[s][:, k * UC:k * UC + w]))
                                   for k in range(KT)], o[:, t * UC:t * UC + w])
                    i.then_inc(sem[unit_done[s]], 1)

                def unit_rows(s, ns, tiles, first, last):
                    pe.wait_ge(*E.at(split_done[s], ns + 1))
                    for t in range(TT):
                        for j, (xh, xl) in enumerate(tiles):
                            ah, al = xh[:, t * P:(t + 1) * P], xl[:, t * P:(t + 1) * P]
                            o = [y_ps[:, t, q * 512:(q + 1) * 512] for q in range(2)]
                            wh, wl = ([w[s][:, j * D + q * 512:j * D + (q + 1) * 512] for q in range(2)]
                                      for w in (w_hi, w_lo))
                            for q in range(2):
                                mm(o[q], ah, wh[q], first and j == 0, False)
                                mm(o[q], ah, wl[q], False, False)
                            for q in range(2):
                                i = mm(o[q], al, wh[q], False, last and j == 1)
                        if last and t == 0:
                            i.then_inc(sem["y_half"], 1)
                    i.then_inc(sem[unit_done[s]], 1)

                def rows_transposed(p):
                    for t in range(TT):
                        pe.wait_ge(s_con, 16)
                        pe.wait_ge(*E.at("xn_ready", 2 * p + t + 1))
                        for k in range(KT):
                            i = t_.transpose(rows_of_t[:, k, t * P:(t + 1) * P], w3[:, t, k * P:(k + 1) * P], ident)
                            if t == TT - 1 and k % 2 == 1:
                                i.then_inc(sem["xt_ready"], 1)

                hid_tiles = [(hid_hi[:, j * S:(j + 1) * S], hid_lo[:, j * S:(j + 1) * S]) for j in range(2)]

                def ffn_up(f, i):
                    (g_, g, gs), (u_, u, us), _, _ = ffn_base(f)
                    fill = (FI_F1, FI_F2)[f] if isinstance(i, int) and i == 0 else None
                    pe.wait_ge(*E.at("hid_done", f * FU + i))
                    unit_feature(g_, g + i, gs + i, bank(4), fill)
                    unit_feature(u_, u + i, us + i, bank(5))

                def ffn_down(f, i, first, last):
                    d_, _, ds = ffn_base(f)[2]
                    if last:
                        (d_, _, ds), i_ = ffn_base(f)[3], 0
                    else:
                        i_ = i
                    pe.wait_ge(*E.at("hid_split", f * FU + 1 + i))
                    unit_rows(d_, ds + i_, hid_tiles, first, last)

                def ffn(f):
                    ffn_up(f, 0)
                    ffn_up(f, 1)
                    ffn_down(f, 0, True, False)
                    with pe.Fori(2, FU) as i:
                        ffn_up(f, i)
                        ffn_down(f, i - 1, False, False)
                        pe.wait_ge(s_con, 16)
                    ffn_down(f, FU - 1, False, True)

                pe.wait_ge(s_con, 16)
                pe.wait_ge(*E.at("h_done", 0))
                rows_transposed(0)
                ffn(0)
                rows_transposed(1)

                def token_unit(m, fill=None):
                    s, n, ns = mid(m)
                    if m >= 2:
                        pe.wait_ge(*E.at("proj_done", m - 1))
                    unit_tokens(s, n, ns, bank(m % 2), IN_W[m], fill)

                s, n, ns = mid(0)
                unit_feature(s, n, ns, bank(0), FI_MIX)
                token_unit(1)
                pe.wait_ge(s_con, 16)
                pe.wait_ge(*E.at("s5_w_done", 1))
                pe.wait_ge(s_con, 16)
                pe.wait_ge(*E.at("x_split", FILL[FI_MIX] + KT))
                for q in range(2):
                    for g in range(PAIRS):
                        i = t_.transpose(bank(4 + 2 * q + g // 4)[:, (g % 4) * P:(g % 4 + 1) * P],
                                         s_w[q][:, g].rearrange("p j c -> p (j c)"), ident)
                i.then_inc(sem["s5_t"], 1)
                pe.wait_ge(*E.at("s5_u_dve", 1))
                token_unit(2)
                pe.wait_ge(*E.at("s5_c_done", 1))
                for g in range(PAIRS):
                    for q in range(2):
                        i = mm(k_ps[:, g, :], s_b4[q][:, g], s_c[q][:, g, 0:CH], q == 0, q == 1)
                i.then_inc(sem["s5_k"], 1)
                token_unit(3)
                pe.wait_ge(*E.at("s5_lb_act", 1))
                pe.wait_ge(*E.at("s5_lb_dve", 1))
                pe.wait_ge(*E.at("s5_u_dve", 1))
                for q in range(2):
                    for g in range(PAIRS):
                        i = mm(bank(4 + q)[:, g * NCH:(g + 1) * NCH], s_lb[:, q, g], s_u[:, g], True, True)
                i.then_inc(sem["s5_v"], 1)
                pe.wait_ge(s_con, 16)
                pe.wait_ge(*E.at("mla_xn", 1))
                for t in range(TT):
                    for k in range(2):
                        t_.transpose(bank(6)[0:QK_T, k * S + t * P:k * S + (t + 1) * P],
                                     pr3[:, t, I_CQ + k * QK_T:I_CQ + (k + 1) * QK_T], ident)
                    i = t_.transpose(bank(7)[:, t * P:(t + 1) * P], pr3[:, t, I_CKV:I_CKV + P], ident)
                i.then_inc(sem["mla_t1"], 1)
                token_unit(4)
                pe.wait_ge(*E.at("mla_t1c", 1))
                pe.wait_ge(*E.at("s5_t0_act", 1))
                pe.wait_ge(*E.at("s5_t0_dve", 1))
                for t in range(TT):
                    for k in range(2):
                        mm(bank(2 + t)[:, 0:384], cq_t[0:QK_T, k, t * P:(t + 1) * P],
                           pmat[0:QK_T, W_UQ + k * 384:W_UQ + (k + 1) * 384], k == 0, k == 1)
                    i = mm(bank(6 + t), ckv_t[:, t * P:(t + 1) * P], pmat[:, W_UKV:W_UKV + 512], True, True)
                i.then_inc(sem["mla_qkv"], 1)
                token_unit(5)
                pe.wait_ge(*E.at("s5_x", 1))
                for g in range(PAIRS):
                    o = bank(4)[:, g * NCH:(g + 1) * NCH]
                    for q in range(2):
                        mm(o, s_c[q][:, g, 1:CH + 1], s_x[q][:, g, 0:NCH], q == 0, False)
                    i = mm(o, s_t0[:, g], s_u[:, g], False, True)
                i.then_inc(sem["s5_y"], 1)
                token_unit(6)
                pe.wait_ge(s_con, 16)
                pe.wait_ge(*E.at("mla_nope", 1))
                pe.wait_ge(s_con, 16)
                pe.wait_ge(*E.at("mla_tok", 1))
                for src, b0 in ((q_tok, 2), (k_tok, 6)):
                    for hh in range(H):
                        for t in range(TT):
                            i = t_.transpose(v3(bank(b0, 2), "p (h s) -> p h s", h=H)[0:MLA_D, hh, t * P:(t + 1) * P],
                                             src[:, t, hh], ident)
                i.then_inc(sem["mla_t2"], 1)
                token_unit(7)
                def scores(g):
                    for hh in range(H):
                        for o, w, at in ((s1[:, hh], S, P), (s0[:, hh], P, 0)):
                            i = mm(o, head_q(g, hh)[:, at:at + P], head_k(g, hh)[:, 0:w], True, g != 3)
                            if g == 3:
                                i = mm(o, ident[:, 32 * hh:32 * hh + 1].to_broadcast([P, P]), ncum[:, 0:w], False, True)
                    i.then_inc(sem["att_s"], 1)

                def probs_transposed(g):
                    pe.wait_ge(s_con, 16)
                    pe.wait_ge(*E.at("att_exp", POS[g] + 1))
                    for hh in range(H):
                        for b, at in ((5, hh * S), (6, hh * S + P), (7, 1024 + hh * P)):
                            i = t_.transpose(bank(b)[:, hh * P:(hh + 1) * P], probs[:, at:at + P], ident)
                    i.then_inc(sem["att_t"], 1)

                def times_values(g):
                    pe.wait_ge(*E.at("att_tc_act", POS[g] + 1))
                    pe.wait_ge(*E.at("att_tc_dve", POS[g] + 1))
                    for hh in range(H):
                        mm(o_ps[0][:, hh], probs_t[:, 1024 + hh * P:1024 + (hh + 1) * P], head_v(g, 0, hh), True, True)
                        for t in range(TT):
                            i = mm(o_ps[1][:, hh], probs_t[:, t * 512 + hh * P:t * 512 + (hh + 1) * P],
                                   head_v(g, t, hh), t == 0, t == 1)
                    i.then_inc(sem["att_pv"], 1)

                pe.wait_ge(*E.at("mla_qt", 1))
                pe.wait_ge(*E.at("mla_kt", 1))
                pe.wait_ge(*E.at("s5_yc", 1))
                scores(0)
                pe.wait_ge(*E.at("s5_sc_act", 1))
                pe.wait_ge(*E.at("s5_sc_dve", 1))
                for q in range(2):
                    for k in range(2):
                        i = mm(bank(5)[:, q * S:(q + 1) * S], pmat[:, W_GLU + k * 256 + q * P:W_GLU + k * 256 + (q + 1) * P],
                               s_yt[:, k], k == 0, k == 1)
                i.then_inc(sem["s5_z"], 1)
                token_unit(8)
                pe.wait_ge(s_con, 16)
                pe.wait_ge(*E.at("nsa_rope", 1))
                pe.wait_ge(s_con, 16)
                pe.wait_ge(*E.at("fox_e", 1))
                for hh in range(H):
                    for t in range(TT):
                        t_.transpose(v3(bank(2, 2), "p (h s) -> p h s", h=H)[0:HD, hh, t * P:(t + 1) * P],
                                     pr3[:, t, I_NQ + hh * HD:I_NQ + (hh + 1) * HD], ident)
                for q, (b, at) in enumerate(((6, I_KC), (6, I_VC), (7, I_KSL), (7, I_KW))):
                    for t in range(TT):
                        i = t_.transpose(bank(b)[0:HD, (q % 2) * S + t * P:(q % 2) * S + (t + 1) * P],
                                         pr3[:, t, at:at + HD], ident)
                i.then_inc(sem["nsa_t"], 1)

                def phi_unit(m):
                    s, n, _ = mid(m)
                    q = m - M_PHI
                    pe.wait_ge(*E.at(raw_in[s], 16 * (n + 1)))
                    for k in range(CMP_KT):
                        i = mm(bank(0)[:, q * 16:q * 16 + NC_CMP], raw[s][:, k * P:(k + 1) * P], bl[:, q // 2, k],
                               k == 0, k == CMP_KT - 1)
                    i.then_inc(sem[unit_done[s]], 1)

                def kv_unit(m):
                    s, n, ns = mid(m)
                    q = KV_UNITS.index(m)
                    if q == 0:
                        pe.wait_ge(*E.at("proj_done", 8))
                    elif q == 1:
                        pe.wait_ge(*E.at("s5_out", 1))
                    elif q == 2:
                        pe.wait_ge(*E.at("phi_x", 1))
                    else:
                        pe.wait_ge(*E.at("xkv_done", q - 1))
                    if q < 4:
                        unit_feature(s, n, ns, bank(KV_BANK[q]), FI_MEM if q == 0 else None)
                    else:
                        unit_tokens(s, n, ns, bank(KV_BANK[q]), UC)

                kv_unit(9)
                pe.wait_ge(s_con, 16)
                pe.wait_ge(*E.at("s5_zt", 1))
                pe.wait_ge(s_con, 16)
                pe.wait_ge(*E.at("nsa_tc_act", 1))
                pe.wait_ge(s_con, 16)
                pe.wait_ge(*E.at("nsa_tc_dve", 1))
                probs_transposed(0)
                pe.wait_ge(*E.at("blocks_done", 1))
                pe.wait_ge(*E.at("proj_done", 9))
                phi_unit(10)
                times_values(0)
                pe.wait_ge(*E.at("fox_lf", 1))
                mm(bank(5)[:, 0:P], lf[:, 0], tri, True, True)
                mm(bank(5)[:, P:S], lf[:, 0], ones, True, False)
                mm(bank(5)[:, P:S], lf[:, 1], tri, False, True)
                mm(bank(5)[:, 256:260], tri, lf[:, 0, 0:P:32], True, True)
                mm(bank(5)[:, 260:264], ones, lf[:, 0, 0:P:32], True, False)
                i = mm(bank(5)[:, 260:264], tri, lf[:, 1, 0:P:32], False, True)
                i.then_inc(sem["fox_cum"], 1)
                pe.wait_ge(*E.at("s5_sq", 1))
                pe.wait_ge(*E.at("xkv_done", 1))
                for t in range(TT):
                    for k in range(2):
                        i = mm(bank(1)[:, S + t:S + t + 1], s_tmp[2][:, k * S + t * P:k * S + (t + 1) * P], ones[:, 0:1],
                               k == 0, k == 1)
                i.then_inc(sem["s5_ss"], 1)
                phi_unit(11)

                def fox_heads(at, b, name):
                    for hh in range(H):
                        for t in range(TT):
                            i = t_.transpose(v3(bank(b, 2), "p (h s) -> p h s", h=H)[0:HD, hh, t * P:(t + 1) * P],
                                             pr3[:, t, at + hh * HD:at + (hh + 1) * HD], ident)
                    i.then_inc(sem[name], 1)

                fox_heads(I_FQ, 6, "fox_tq")
                pe.wait_ge(s_con, 16)
                pe.wait_ge(*E.at("att_out", 1))
                fox_heads(I_FK, 2, "fox_tk")
                pe.wait_ge(*E.at("s5_rstd", 1))
                for t in range(TT):
                    i = mm(bank(1)[:, t * P:(t + 1) * P], s5_r[:, t:t + 1].to_broadcast([P, P]), ident, True, True)
                i.then_inc(sem["s5_rstd_all"], 1)
                phi_unit(12)
                pe.wait_ge(*E.at("fox_nc", 1))
                pe.wait_ge(*E.at("fox_qt", 1))
                pe.wait_ge(*E.at("fox_kt", 1))
                scores(3)
                phi_unit(13)
                kv_unit(14)
                probs_transposed(3)
                kv_unit(15)
                times_values(3)
                pe.wait_ge(*E.at("phi_hid", 1))
                for f in range(2):
                    mm(bank(5)[0:HD, 0:NC_CMP], pmat[:, W_PHI2 + f * HD:W_PHI2 + (f + 1) * HD],
                       hx[:, f * NC_CMP:(f + 1) * NC_CMP], f == 0, f == 1)
                for f in (2, 3):
                    i = mm(bank(5)[0:NC_CMP, 64:128], hx[:, f * NC_CMP:(f + 1) * NC_CMP],
                           pmat[:, W_PHI2 + f * HD:W_PHI2 + (f + 1) * HD], f == 2, f == 3)
                i.then_inc(sem["phi_out"], 1)
                kv_unit(16)
                pe.wait_ge(*E.at("att_out", 2))
                scores(1)
                pe.wait_ge(*E.at("phi_c", 1))
                for t in range(TT):
                    for hh in range(H):
                        i = mm(c_ps[:, t * H + hh, 0:NC_CMP], qn[0:HD, hh, t * P:(t + 1) * P], kct[0:HD, 0:NC_CMP],
                               True, True)
                i.then_inc(sem["cmp_s"], 1)
                kv_unit(17)
                pe.wait_ge(s_con, 16)
                pe.wait_ge(*E.at("cmp_x", 1))
                probs_transposed(1)
                kv_unit(18)
                pe.wait_ge(*E.at("nsa_v", 1))
                times_values(1)
                pe.wait_ge(s_con, 16)
                pe.wait_ge(*E.at("cmp_p", 1))
                for hh in range(H):
                    for t in range(TT):
                        i = t_.transpose(v3(bank(6, 2), "p (h s) -> p h s", h=H)[0:NC_CMP, hh, t * P:(t + 1) * P],
                                         cp[:, t * H + hh], ident)
                i.then_inc(sem["cmp_t"], 1)
                kv_unit(19)
                pe.wait_ge(*E.at("att_out", 3))
                scores(2)
                pe.wait_ge(*E.at("cmp_tc", 1))
                for t in range(TT):
                    for hh in range(H):
                        i = mm(bank(5)[:, (t * H + hh) * HD:(t * H + hh + 1) * HD],
                               probs_t[0:NC_CMP, hh * S + t * P:hh * S + (t + 1) * P], vct[0:NC_CMP], True, True)
                i.then_inc(sem["cmp_o"], 1)
                kv_unit(20)
                pe.wait_ge(s_con, 16)
                pe.wait_ge(*E.at("cmp_done", 1))
                probs_transposed(2)
                times_values(2)

                pe.wait_ge(s_con, 16)
                pe.wait_ge(*E.at("grp_xn", 1))
                for k in range(6):
                    for t in range(TT):
                        i = t_.transpose(rows_of_t[:, k, t * P:(t + 1) * P],
                                         mix_out[:, t * 768 + k * P:t * 768 + (k + 1) * P], ident)
                    if k % 2 == 1:
                        i.then_inc(sem["grp_t"], 1)
                pe.wait_ge(*E.at("xkv_done", 8))
                pe.wait_ge(*E.at("att_out", 4))
                for q in range(4):
                    s, n, ns = mid(M_OUT + q)
                    pe.wait_ge(*E.at("x_split", FILL[FI_MO] + 2 * q + 2))
                    unit_rows(s, ns, [(xh3[:, k], xl3[:, k]) for k in MO_ORDER[2 * q:2 * q + 2]], q == 0, q == 3)
                pe.wait_ge(*E.at("x_split", FILL[FI_MO] + KT))
                rows_transposed(2)

                def xa_scores(q):
                    pe.wait_ge(*E.at("xq_done", q + 1))
                    for t in range(TT):
                        for k in range(2):
                            i = mm(bank(6 + q % 2)[:, t * S:(t + 1) * S], xq[:, 2 * q + k, t * P:(t + 1) * P],
                                   xk[:, 2 * q + k], k == 0, k == 1)
                    i.then_inc(sem["xs"], 1)

                def xa_transposed(q):
                    pe.wait_ge(s_con, 16)
                    pe.wait_ge(*E.at("xp", q + 1))
                    for t in range(TT):
                        for m_ in range(TT):
                            i = t_.transpose(bank(2 + q % 2)[:, m_ * S + t * P:m_ * S + (t + 1) * P],
                                             probs[:, (q % 2) * 512 + t * S + m_ * P:(q % 2) * 512 + t * S + (m_ + 1) * P],
                                             ident)
                    i.then_inc(sem["xt"], 1)

                def xa_values(q):
                    pe.wait_ge(*E.at("xtc", q + 1))
                    if q >= 2:
                        pe.wait_ge(*E.at("xoc", q - 1))
                    for d in range(2):
                        for m_ in range(TT):
                            i = mm(bank(q % 2)[:, d * S:(d + 1) * S], xv[:, m_, q * UC + d * P:q * UC + (d + 1) * P],
                                   probs_t[:, (q % 2) * 512 + m_ * S:(q % 2) * 512 + (m_ + 1) * S], m_ == 0, m_ == 1)
                    i.then_inc(sem["xo"], 1)

                for q in range(4):
                    s, n, ns = mid(M_Q + q)
                    unit_feature(s, n, ns, bank(4 + q % 2), FI_XA if q == 0 else None)
                    xa_scores(q)
                    if q >= 1:
                        xa_transposed(q - 1)
                    if q >= 2:
                        xa_values(q - 2)
                xa_transposed(3)
                xa_values(2)
                xa_values(3)
                pe.wait_ge(*E.at("xoc", 4))
                for q in range(4):
                    s, n, ns = mid(M_O + q)
                    pe.wait_ge(*E.at("x_split", FILL[FI_XO] + q + 1))
                    unit_rows(s, ns, [(xh3[:, 2 * q + k], xl3[:, 2 * q + k]) for k in range(2)], q == 0, q == 3)

                rows_transposed(3)
                ffn(1)
                pe.wait_ge(s_con, 16)


def pack(inputs):
    g = {k: np.ascontiguousarray(v) for k, v in inputs.items()}
    w = np.zeros((DEPTH * N_UNITS, P, UNIT), np.float32)

    def tall(m):
        u = np.zeros((P, KT, UC), np.float32)
        u[:, :, :m.shape[1]] = m.reshape(KT, P, -1).transpose(1, 0, 2)
        return u.reshape(P, UNIT)

    def wide(m):
        return m.reshape(2, P, D).transpose(1, 0, 2).reshape(P, UNIT)

    for l in range(DEPTH):
        at = l * N_UNITS

        def put(u):
            nonlocal at
            w[at] = u
            at += 1

        def ffn(n):
            gate, up, down = (g[f"ffn{n}_w_{x}"][l] for x in ("gate", "up", "down"))
            c = [slice(i * UC, (i + 1) * UC) for i in range(FU)]
            for i in range(FU + 1):
                if i < FU:
                    put(tall(gate[:, c[i]]))
                    put(tall(up[:, c[i]]))
                if i:
                    put(wide(down[c[i - 1]]))

        ffn(1)
        for ranges in IN_UNITS:
            put(tall(np.concatenate([g["mix_w_in"][l][:, a:b] for a, b in ranges], 1)))
        put(tall(g["xa_w_kv"][l][:, 0:UC]))
        for j in range(2):
            for f in range(2):
                u = g["nsa_phi_w1"][l, j][:, f * P:(f + 1) * P]
                put(u.reshape(CMP_KT, P, P).transpose(1, 0, 2).reshape(P, UNIT))
        for q in range(1, 8):
            put(tall(g["xa_w_kv"][l][:, q * UC:(q + 1) * UC]))
        for q in (3, 0, 1, 2):
            put(wide(g["mix_w_out"][l][q * UC:(q + 1) * UC]))
        for q in range(4):
            put(tall(g["xa_w_q"][l][:, q * UC:(q + 1) * UC]))
        for q in range(4):
            put(wide(g["xa_w_o"][l][q * UC:(q + 1) * UC]))
        ffn(2)
        assert at == (l + 1) * N_UNITS

    cols = np.zeros((DEPTH + 1, P, NCOL), np.float32)
    mats = np.zeros((DEPTH + 1, P, NMAT), np.float32)
    post = np.zeros((DEPTH * 4, D), np.float32)

    def col(a, n):
        return a.reshape(n, P).T

    for l in range(DEPTH):
        c, m = cols[l], mats[l]
        for base, name in ((C_FFN1, "ffn1_pre_g"), (C_MIX, "mix_pre_g"), (C_XA, "xa_pre_g"),
                           (C_MEM, "xa_mem_g"), (C_FFN2, "ffn2_pre_g"), (C_GRP, "mix_group_g")):
            c[:, base:base + KT] = col(g[name][l], KT)
        c[:, C_GLUB:C_GLUB + 2] = col(g["s5_glu_b"][l], 2)
        c[:, C_PHIB:C_PHIB + 4] = col(g["nsa_phi_b1"][l], 4)
        c[:QK_T, C_QN:C_QN + 2] = g["mla_q_norm_g"][l].reshape(2, QK_T).T
        c[:, C_KVN] = g["mla_kv_norm_g"][l]
        c[:, C_LR:C_LR + PAIRS] = col(g["s5_lambda_re"][l], PAIRS)
        c[:, C_LI:C_LI + PAIRS] = col(g["s5_lambda_im"][l], PAIRS)
        for q in range(2):
            c[q * ST5:(q + 1) * ST5, C_LDT:C_LDT + PAIRS] = g["s5_log_dt"][l][None, q::2]
        c[:, C_POS:C_POS + 2 * CMP_KT] = col(g["nsa_cmp_pos"][l], 2 * CMP_KT)
        c[:, C_GB:C_GB + 3 * H] = g["nsa_gate_b"][l][None]
        c[:, C_FB:C_FB + H] = g["fox_f_b"][l][None]
        m[:QK_T, W_UQ:W_UQ + 768] = g["mla_w_uq"][l].reshape(2, QK_T, 384).transpose(1, 0, 2).reshape(QK_T, 768)
        m[:, W_UKV:W_UKV + 512] = g["mla_w_ukv"][l]
        m[:, W_GLU:W_GLU + 512] = g["s5_glu_w"][l].reshape(2, P, 256).transpose(1, 0, 2).reshape(P, 512)
        m[:, W_PHI2:W_PHI2 + 256] = g["nsa_phi_w2"][l].reshape(4, P, HD).transpose(1, 0, 2).reshape(P, 256)
        for q in range(G5):
            pair, e = q // 2, q % 2
            rows, at = slice(e * ST5, (e + 1) * ST5), pair * C2 + e * C5
            m[rows, W_BR + at:W_BR + at + C5] = g["s5_b_re"][l, q]
            m[rows, W_BI + at:W_BI + at + C5] = g["s5_b_im"][l, q]
            m[rows, W_CR + at:W_CR + at + C5] = g["s5_c_re"][l, q].T
            m[rows, W_CI + at:W_CI + at + C5] = g["s5_c_im"][l, q].T
            for j in range(CH):
                for i in range(C5):
                    m[j * C2 + e * C5 + i, W_D + at + i] = g["s5_d"][l, q, i]
        for n, name in enumerate(("ffn1_post_g", "mix_post_g", "xa_post_g", "ffn2_post_g")):
            post[l * 4 + n] = g[name][l]
    return {"x": g["x"].reshape(S, D), "mem": g["mem"].reshape(S, D), "weights": w, "cols": cols,
            "mats": mats, "post": post, "consts": constants()}


def kernel(**inputs):
    import concourse.bacc as bacc
    from concourse.bass_utils import run_bass_kernel_spmd

    nc = bacc.Bacc("TRN2", target_bir_lowering=False, num_devices=1)
    arrays = {f"in_{k}": v for k, v in pack(inputs).items()}
    args = [nc.dram_tensor(k, v.shape, F32, kind="ExternalInput").ap() for k, v in arrays.items()]
    out = nc.dram_tensor("out", (S, D), F32, kind="ExternalOutput").ap()
    mem_scratch = nc.dram_tensor("mem_scratch", (P, KT * S), F32).ap()
    program(nc, *args, out, mem_scratch)
    r = run_bass_kernel_spmd(nc, [arrays], core_ids=[0])
    return r.results[0]["out"].reshape(1, S, D)
```
